# Optimizing a Trainium2 kernel written in Bass

```python
import jax, jax.numpy as jnp
from jax import lax
import numpy as np

D_MODEL = 1024
BATCH = 1
SEQ = 256
DEPTH = 2

HEAD_DIM = 64
EPS = 1e-6
N_BRANCH = 3
CONV_WIDTH = D_MODEL
CONV_KERNEL = 31
RET_HEADS = 4
RET_QK_DIM = D_MODEL // RET_HEADS
RET_V_DIM = 2 * RET_QK_DIM
RET_CHUNK = 128
RET_THETA = 10000.0
ATTN_HEADS = D_MODEL // HEAD_DIM
ATTN_KV_HEADS = 4
ATTN_WINDOW = 128
ATTN_BLOCK = 128
ROPE_THETA = 500000.0
ROPE_DIM = HEAD_DIM // 4

IN_SPLITS = (
    2 * CONV_WIDTH,
    CONV_WIDTH,
    RET_HEADS * RET_QK_DIM,
    RET_HEADS * RET_QK_DIM,
    RET_HEADS * RET_V_DIM,
    RET_HEADS * RET_V_DIM,
    ATTN_HEADS * HEAD_DIM,
    ATTN_KV_HEADS * HEAD_DIM,
    ATTN_KV_HEADS * HEAD_DIM,
    ATTN_HEADS * HEAD_DIM,
    N_BRANCH * D_MODEL,
)
IN_WIDTH = sum(IN_SPLITS)


def rms_norm(x, g):
    xf = x.astype(jnp.float32)
    y = xf * lax.rsqrt(jnp.mean(xf * xf, axis=-1, keepdims=True) + EPS) * g.astype(jnp.float32)
    return y.astype(x.dtype)

def rotary(x, positions, theta, rot_dim):
    half = rot_dim // 2
    inv_freq = theta ** (-jnp.arange(half, dtype=jnp.float32) / half)
    ang = positions.astype(jnp.float32)[:, None] * inv_freq[None, :]
    cos = jnp.cos(ang)[:, None, :]
    sin = jnp.sin(ang)[:, None, :]
    xf = x.astype(jnp.float32)
    x1 = xf[..., :half]
    x2 = xf[..., half:rot_dim]
    out = jnp.concatenate([x1 * cos - x2 * sin, x2 * cos + x1 * sin, xf[..., rot_dim:]], axis=-1)
    return out.astype(x.dtype)

def conv_module(u_glu, gate, dw, db, ln_g, ln_b):
    a, b = jnp.split(u_glu, 2, axis=-1)
    v = a * jax.nn.sigmoid(b)
    y = lax.conv_general_dilated(
        v, dw[:, None, :].astype(v.dtype), window_strides=(1,),
        padding=[(CONV_KERNEL // 2, CONV_KERNEL // 2)],
        dimension_numbers=('NWC', 'WIO', 'NWC'),
        feature_group_count=CONV_WIDTH) + db.astype(v.dtype)
    yf = y.astype(jnp.float32)
    mu = jnp.mean(yf, axis=-1, keepdims=True)
    var = jnp.mean(jnp.square(yf - mu), axis=-1, keepdims=True)
    yf = (yf - mu) * lax.rsqrt(var + EPS) * ln_g.astype(jnp.float32) + ln_b.astype(jnp.float32)
    y = jax.nn.silu(yf).astype(v.dtype)
    return y * jax.nn.silu(gate)

def retention_one_direction(q, k, v, log_gamma, inclusive):
    B, H, S, dk = q.shape
    dv = v.shape[-1]
    C = RET_CHUNK
    n = S // C
    qc = q.reshape(B, H, n, C, dk)
    kc = k.reshape(B, H, n, C, dk)
    vc = v.reshape(B, H, n, C, dv)
    idx = jnp.arange(C, dtype=jnp.float32)
    diff = idx[:, None] - idx[None, :]
    mask = (diff >= 0) if inclusive else (diff > 0)
    lg = log_gamma[:, None, None]
    decay_inner = jnp.where(mask[None], jnp.exp(lg * jnp.where(mask, diff, 0.0)[None]), 0.0)
    scores = jnp.einsum('bhnid,bhnjd->bhnij', qc, kc) * decay_inner[None, :, None]
    inner = jnp.einsum('bhnij,bhnjv->bhniv', scores, vc)
    q_decay = jnp.exp(log_gamma[:, None] * (idx[None, :] + 1.0))[None, :, :, None]
    k_decay = jnp.exp(log_gamma[:, None] * (C - 1.0 - idx[None, :]))[None, :, :, None]
    chunk_decay = jnp.exp(log_gamma * C)[None, :, None, None]

    def step(state, xs):
        q_t, k_t, v_t = xs
        cross = jnp.einsum('bhcd,bhdv->bhcv', q_t * q_decay, state)
        state = chunk_decay * state + jnp.einsum('bhcd,bhcv->bhdv', k_t * k_decay, v_t)
        return state, cross

    state0 = jnp.zeros((B, H, dk, dv), jnp.float32)
    xs = (jnp.moveaxis(qc, 2, 0), jnp.moveaxis(kc, 2, 0), jnp.moveaxis(vc, 2, 0))
    _, cross = lax.scan(step, state0, xs)
    out = inner + jnp.moveaxis(cross, 0, 2)
    return out.reshape(B, H, S, dv)

def retention_branch(q, k, v, gate, ret_decay, positions):
    B, S, _ = q.shape
    q = rotary(q.reshape(B, S, RET_HEADS, RET_QK_DIM), positions, RET_THETA, RET_QK_DIM)
    k = rotary(k.reshape(B, S, RET_HEADS, RET_QK_DIM), positions, RET_THETA, RET_QK_DIM)
    qf = jnp.transpose(q, (0, 2, 1, 3)).astype(jnp.float32)
    kf = jnp.transpose(k, (0, 2, 1, 3)).astype(jnp.float32) * (RET_QK_DIM ** -0.5)
    vf = jnp.transpose(v.reshape(B, S, RET_HEADS, RET_V_DIM), (0, 2, 1, 3)).astype(jnp.float32)
    log_gamma = -jnp.exp(ret_decay.astype(jnp.float32))
    fwd = retention_one_direction(qf, kf, vf, log_gamma[0], True)
    bwd = retention_one_direction(qf[:, :, ::-1], kf[:, :, ::-1], vf[:, :, ::-1], log_gamma[1], False)[:, :, ::-1]
    o = fwd + bwd
    mu = jnp.mean(o, axis=-1, keepdims=True)
    var = jnp.mean(jnp.square(o - mu), axis=-1, keepdims=True)
    o = (o - mu) * lax.rsqrt(var + EPS)
    o = jnp.transpose(o, (0, 2, 1, 3)).reshape(B, S, RET_HEADS * RET_V_DIM).astype(gate.dtype)
    return o * jax.nn.silu(gate)

def window_attention_branch(q, k, v, gate, q_norm_g, k_norm_g, sink, positions):
    B, S, _ = q.shape
    G = ATTN_HEADS // ATTN_KV_HEADS
    T = ATTN_BLOCK
    nb = S // T
    q = rms_norm(q.reshape(B, S, ATTN_HEADS, HEAD_DIM), q_norm_g)
    k = rms_norm(k.reshape(B, S, ATTN_KV_HEADS, HEAD_DIM), k_norm_g)
    q = rotary(q, positions, ROPE_THETA, ROPE_DIM)
    k = rotary(k, positions, ROPE_THETA, ROPE_DIM)
    v = v.reshape(B, S, ATTN_KV_HEADS, HEAD_DIM)
    qb = q.reshape(B, nb, T, ATTN_KV_HEADS, G, HEAD_DIM).astype(jnp.float32)
    pad = ((0, 0), (T, T), (0, 0), (0, 0))
    kb = jnp.pad(k, pad).reshape(B, nb + 2, T, ATTN_KV_HEADS, HEAD_DIM)
    vb = jnp.pad(v, pad).reshape(B, nb + 2, T, ATTN_KV_HEADS, HEAD_DIM)
    kwin = jnp.concatenate([kb[:, :-2], kb[:, 1:-1], kb[:, 2:]], axis=2).astype(jnp.float32)
    vwin = jnp.concatenate([vb[:, :-2], vb[:, 1:-1], vb[:, 2:]], axis=2).astype(jnp.float32)
    s = jnp.einsum('bnqhgd,bnjhd->bhgnqj', qb, kwin) * (HEAD_DIM ** -0.5)
    blk = jnp.arange(nb)[:, None, None]
    qpos = blk * T + jnp.arange(T)[None, :, None]
    kpos = (blk - 1) * T + jnp.arange(3 * T)[None, None, :]
    valid = (jnp.abs(kpos - qpos) <= ATTN_WINDOW) & (kpos >= 0) & (kpos < S)
    s = jnp.where(valid, s, -1e30)
    sink_l = sink.astype(jnp.float32).reshape(ATTN_KV_HEADS, G, 1, 1, 1)
    m = jnp.maximum(jnp.max(s, axis=-1, keepdims=True), sink_l)
    p = jnp.exp(s - m)
    p = p / (jnp.sum(p, axis=-1, keepdims=True) + jnp.exp(sink_l - m))
    o = jnp.einsum('bhgnqj,bnjhd->bnqhgd', p, vwin)
    o = o.reshape(B, S, ATTN_HEADS * HEAD_DIM).astype(gate.dtype)
    return o * jax.nn.silu(gate)

def hybrid_layer(x, positions, norm_g, w_in, b_gate, conv_dw, conv_b, conv_ln_g, conv_ln_b,
                 ret_decay, q_norm_g, k_norm_g, attn_sink, w_conv_out, w_ret_out, w_attn_out, w_out):
    B, S, D = x.shape
    h = rms_norm(x, norm_g)
    z = h @ w_in
    offsets = np.cumsum(IN_SPLITS)[:-1].tolist()
    (c_glu, c_gate, r_q, r_k, r_v, r_gate, a_q, a_k, a_v, a_gate, g_logit) = jnp.split(z, offsets, axis=-1)
    y_conv = conv_module(c_glu, c_gate, conv_dw, conv_b, conv_ln_g, conv_ln_b) @ w_conv_out
    y_ret = retention_branch(r_q, r_k, r_v, r_gate, ret_decay, positions) @ w_ret_out
    y_attn = window_attention_branch(a_q, a_k, a_v, a_gate, q_norm_g, k_norm_g, attn_sink, positions) @ w_attn_out
    g = jax.nn.sigmoid(g_logit + b_gate).reshape(B, S, N_BRANCH, D)
    merged = g[:, :, 0] * y_conv + g[:, :, 1] * y_ret + g[:, :, 2] * y_attn
    return x + merged @ w_out

def first_inputs(seed: int = 0) -> dict:
    key = jax.random.key(seed)
    ks = jax.random.split(key, 18)
    nrm = jax.random.normal
    f32 = jnp.float32
    ret_base = jnp.log(-jnp.log1p(-(2.0 ** (-5.0 - jnp.arange(RET_HEADS, dtype=f32)))))
    return {
        'x': nrm(ks[0], (BATCH, SEQ, D_MODEL), f32),
        'norm_g': 1.0 + 0.02 * nrm(ks[1], (DEPTH, D_MODEL), f32),
        'w_in': nrm(ks[2], (DEPTH, D_MODEL, IN_WIDTH), f32) * D_MODEL ** -0.5,
        'b_gate': 0.1 * nrm(ks[3], (DEPTH, N_BRANCH * D_MODEL), f32),
        'conv_dw': nrm(ks[4], (DEPTH, CONV_KERNEL, CONV_WIDTH), f32) * CONV_KERNEL ** -0.5,
        'conv_b': 0.02 * nrm(ks[5], (DEPTH, CONV_WIDTH), f32),
        'conv_ln_g': 1.0 + 0.02 * nrm(ks[6], (DEPTH, CONV_WIDTH), f32),
        'conv_ln_b': 0.02 * nrm(ks[7], (DEPTH, CONV_WIDTH), f32),
        'ret_decay': ret_base + 0.05 * nrm(ks[8], (DEPTH, 2, RET_HEADS), f32),
        'q_norm_g': 1.0 + 0.02 * nrm(ks[9], (DEPTH, HEAD_DIM), f32),
        'k_norm_g': 1.0 + 0.02 * nrm(ks[10], (DEPTH, HEAD_DIM), f32),
        'attn_sink': 0.5 * nrm(ks[11], (DEPTH, ATTN_HEADS), f32),
        'w_conv_out': nrm(ks[12], (DEPTH, CONV_WIDTH, D_MODEL), f32) * CONV_WIDTH ** -0.5,
        'w_ret_out': nrm(ks[13], (DEPTH, RET_HEADS * RET_V_DIM, D_MODEL), f32) * (RET_HEADS * RET_V_DIM) ** -0.5,
        'w_attn_out': nrm(ks[14], (DEPTH, ATTN_HEADS * HEAD_DIM, D_MODEL), f32) * (ATTN_HEADS * HEAD_DIM) ** -0.5,
        'w_out': nrm(ks[15], (DEPTH, D_MODEL, D_MODEL), f32) * D_MODEL ** -0.5,
    }

def first_block(x, norm_g, w_in, b_gate, conv_dw, conv_b, conv_ln_g, conv_ln_b, ret_decay,
              q_norm_g, k_norm_g, attn_sink, w_conv_out, w_ret_out, w_attn_out, w_out):
    positions = jnp.arange(x.shape[1], dtype=jnp.int32)
    for l in range(DEPTH):
        x = hybrid_layer(x, positions, norm_g[l], w_in[l], b_gate[l], conv_dw[l], conv_b[l],
                         conv_ln_g[l], conv_ln_b[l], ret_decay[l], q_norm_g[l], k_norm_g[l],
                         attn_sink[l], w_conv_out[l], w_ret_out[l], w_attn_out[l], w_out[l])
    return x


DEPTH_2 = 1

GRID_W = 64
CTX_LEN = 256
MIX_WIDTH = D_MODEL
RWKV_WIDTH = MIX_WIDTH // 2
HEAD_SIZE = 64
RWKV_HEADS = RWKV_WIDTH // HEAD_SIZE
FNET_WIDTH = MIX_WIDTH - RWKV_WIDTH
FNET_GROUPS = 8
FNET_GROUP_W = FNET_WIDTH // FNET_GROUPS
DECAY_LORA = 64
ICLR_LORA = 64
GATE_LORA = 128
N_DIR = 2
SHIFT_WIDTH = 3 * RWKV_WIDTH + N_DIR * (DECAY_LORA + ICLR_LORA + GATE_LORA)
IN_WIDTH_2 = SHIFT_WIDTH + FNET_WIDTH
N_EXPERTS = 32
TOP_K = 4
D_FF = D_MODEL
SWIGLU_LIMIT = 7.0
SWIGLU_ALPHA = 1.702
EXPERT_BLOCK = 128
DEEPNORM_ALPHA = (2.0 * DEPTH_2) ** 0.25
DEEPNORM_BETA = (8.0 * DEPTH_2) ** -0.25
LN_EPS = 1e-5
GN_EPS = 64e-5


def layer_norm(u, g, b):
    u32 = u.astype(jnp.float32)
    mean = jnp.mean(u32, -1, keepdims=True)
    var = jnp.mean(jnp.square(u32 - mean), -1, keepdims=True)
    return ((u32 - mean) * lax.rsqrt(var + LN_EPS) * g + b).astype(u.dtype)

def grid_shift(u):
    b_, t, ch = u.shape
    rows = t // GRID_W
    g = u.reshape(b_, rows, GRID_W, ch)
    p = jnp.pad(g, ((0, 0), (1, 1), (1, 1), (0, 0)))
    nb = (p[:, :-2, 1:-1] + p[:, 2:, 1:-1] + p[:, 1:-1, :-2] + p[:, 1:-1, 2:]) * 0.25
    return nb.reshape(b_, t, ch)

def seq_shift(u):
    p = jnp.pad(u, ((0, 0), (1, 1), (0, 0)))
    return (p[:, :-2] + p[:, 2:]) * 0.5

def heads(z):
    return z.reshape(z.shape[:-1] + (RWKV_HEADS, HEAD_SIZE))

def rwkv_prepare(m, w0, w2_decay, a0, a2_iclr, g2_gate, k_k, k_a):
    b_, t, _ = m.shape
    c = RWKV_WIDTH
    r = m[..., :c]
    k = m[..., c:2 * c]
    v = m[..., 2 * c:3 * c]
    o = 3 * c
    wd = m[..., o:o + N_DIR * DECAY_LORA].reshape(b_, t, N_DIR, DECAY_LORA)
    o += N_DIR * DECAY_LORA
    ad = m[..., o:o + N_DIR * ICLR_LORA].reshape(b_, t, N_DIR, ICLR_LORA)
    o += N_DIR * ICLR_LORA
    gd = m[..., o:o + N_DIR * GATE_LORA].reshape(b_, t, N_DIR, GATE_LORA)
    w_log = w0 + jnp.einsum('btdr,drc->btdc', jnp.tanh(wd), w2_decay)
    w = jnp.exp(-jnp.exp(-jax.nn.softplus(-w_log) - 0.5))
    a = jax.nn.sigmoid(a0 + jnp.einsum('btdr,drc->btdc', ad, a2_iclr))
    g = jnp.einsum('btdr,drc->btdc', jax.nn.sigmoid(gd), g2_gate)
    kk = heads(k * k_k)
    kk = kk / jnp.maximum(jnp.sqrt(jnp.sum(jnp.square(kk), -1, keepdims=True)), 1e-12)
    k_d = k[:, :, None] * (1.0 + (a - 1.0) * k_a)
    return heads(r), heads(k_d), heads(v), kk, heads(w), heads(a), g

def wkv_bidir(r, k_d, v, kk, w, a, state0):
    def both(u):
        return jnp.stack([u, jnp.flip(u, 1)], 0)

    def per(u):
        return jnp.stack([u[:, :, 0], jnp.flip(u[:, :, 1], 1)], 0)

    def tm(z):
        return jnp.moveaxis(z, 2, 0)

    xs = (tm(both(r)), tm(per(w)), tm(per(k_d)), tm(both(v)), tm(both(-kk)), tm(per(kk[:, :, None] * a)))

    def step(s, inp):
        r_t, w_t, k_t, v_t, aa_t, bb_t = inp
        sa = jnp.einsum('dbhij,dbhj->dbhi', s, aa_t)
        s = s * w_t[..., None, :] + sa[..., :, None] * bb_t[..., None, :] + v_t[..., :, None] * k_t[..., None, :]
        y_t = jnp.einsum('dbhij,dbhj->dbhi', s, r_t)
        return s, y_t

    state, ys = lax.scan(step, state0, xs)
    ys = jnp.moveaxis(ys, 0, 2)
    y = jnp.stack([ys[0], jnp.flip(ys[1], 1)], axis=2)
    return y, state

def rwkv_output(y, r, k_d, v, g, r_k, gn_g, gn_b):
    b_, t = y.shape[:2]
    mean = jnp.mean(y, -1, keepdims=True)
    var = jnp.mean(jnp.square(y - mean), -1, keepdims=True)
    yn = (y - mean) * lax.rsqrt(var + GN_EPS) * heads(gn_g) + heads(gn_b)
    bonus = jnp.sum(r[:, :, None] * k_d * r_k, -1, keepdims=True) * v[:, :, None]
    return jnp.sum((yn + bonus).reshape(b_, t, N_DIR, RWKV_WIDTH) * g, axis=2)

def fourier_mix(f, w_fno, b_fno):
    b_, t, _ = f.shape
    fg = f.reshape(b_, t, FNET_GROUPS, FNET_GROUP_W).astype(jnp.float32)
    spec = jnp.real(jnp.fft.fft2(fg, axes=(1, 3), norm='ortho'))
    y = jnp.einsum('btgc,gce->btge', spec, w_fno) + b_fno
    return y.reshape(b_, t, FNET_WIDTH)

def token_mixer(h_lat, h_ctx, w_in, mu_shift, w0, w2_decay, a0, a2_iclr, g2_gate, r_k, k_k, k_a,
                gn_g, gn_b, w_fno, b_fno, w_out, need_ctx):
    f32 = jnp.float32
    p_lat = jnp.einsum('btd,de->bte', h_lat, w_in).astype(f32)
    p_ctx = jnp.einsum('btd,de->bte', h_ctx, w_in).astype(f32)
    s_lat, f_lat = p_lat[..., :SHIFT_WIDTH], p_lat[..., SHIFT_WIDTH:]
    s_ctx, f_ctx = p_ctx[..., :SHIFT_WIDTH], p_ctx[..., SHIFT_WIDTH:]
    mu = mu_shift.astype(f32)
    m_lat = s_lat + mu * (grid_shift(s_lat) - s_lat)
    m_ctx = s_ctx + mu * (seq_shift(s_ctx) - s_ctx)
    dp = (w0, w2_decay, a0, a2_iclr, g2_gate, k_k, k_a)
    r_c, k_c, v_c, kk_c, w_c, a_c, g_c = rwkv_prepare(m_ctx, *dp)
    state0 = jnp.zeros((N_DIR, h_ctx.shape[0], RWKV_HEADS, HEAD_SIZE, HEAD_SIZE), f32)
    y_c, state_c = wkv_bidir(r_c, k_c, v_c, kk_c, w_c, a_c, state0)
    r_l, k_l, v_l, kk_l, w_l, a_l, g_l = rwkv_prepare(m_lat, *dp)
    y_l, _ = wkv_bidir(r_l, k_l, v_l, kk_l, w_l, a_l, state_c)
    rw_lat = rwkv_output(y_l, r_l, k_l, v_l, g_l, r_k, gn_g, gn_b)
    out_lat = jnp.concatenate([rw_lat, fourier_mix(f_lat, w_fno, b_fno)], -1) @ w_out.astype(f32)
    out_ctx = None
    if need_ctx:
        rw_ctx = rwkv_output(y_c, r_c, k_c, v_c, g_c, r_k, gn_g, gn_b)
        out_ctx = (jnp.concatenate([rw_ctx, fourier_mix(f_ctx, w_fno, b_fno)], -1) @ w_out.astype(f32)).astype(h_ctx.dtype)
    return out_lat.astype(h_lat.dtype), out_ctx

def moe_ffn(h, w_router, b_router, w1, b1, w2, b2):
    f32 = jnp.float32
    n_tok = h.shape[0]
    logits = h.astype(f32) @ w_router.astype(f32) + b_router.astype(f32)
    top_val, top_idx = lax.top_k(logits, TOP_K)
    gates = jax.nn.softmax(top_val, axis=-1)
    n_assign = n_tok * TOP_K
    e_flat = top_idx.reshape(-1).astype(jnp.int32)
    tok_flat = jnp.repeat(jnp.arange(n_tok, dtype=jnp.int32), TOP_K)
    g_flat = gates.reshape(-1)
    order = jnp.argsort(e_flat)
    e_s, tok_s, g_s = e_flat[order], tok_flat[order], g_flat[order]
    counts = jnp.bincount(e_flat, length=N_EXPERTS).astype(jnp.int32)
    starts = jnp.cumsum(counts) - counts
    padded = (counts + EXPERT_BLOCK - 1) // EXPERT_BLOCK * EXPERT_BLOCK
    pends = jnp.cumsum(padded)
    pstarts = pends - padded
    slot = pstarts[e_s] + jnp.arange(n_assign, dtype=jnp.int32) - starts[e_s]
    n_blocks = -(-n_assign // EXPERT_BLOCK) + N_EXPERTS
    n_slots = n_blocks * EXPERT_BLOCK
    slot_tok = jnp.zeros((n_slots,), jnp.int32).at[slot].set(tok_s)
    slot_gate = jnp.zeros((n_slots,), f32).at[slot].set(g_s)
    block_start = jnp.arange(n_blocks, dtype=jnp.int32) * EXPERT_BLOCK
    block_e = jnp.minimum(jnp.searchsorted(pends, block_start, side='right'), N_EXPERTS - 1)

    def expert_block(args):
        tok_b, e = args
        xb = h[tok_b]
        u = xb @ w1[e] + b1[e]
        glu = jnp.minimum(u[:, 0::2], SWIGLU_LIMIT)
        lin = jnp.clip(u[:, 1::2], -SWIGLU_LIMIT, SWIGLU_LIMIT)
        act = glu * jax.nn.sigmoid(SWIGLU_ALPHA * glu) * (lin + 1.0)
        return act @ w2[e] + b2[e]

    y = lax.map(expert_block, (slot_tok.reshape(n_blocks, EXPERT_BLOCK), block_e))
    out = jnp.zeros((n_tok, h.shape[1]), f32).at[slot_tok].add(slot_gate[:, None] * y.reshape(n_slots, -1))
    return out.astype(h.dtype)

def second_inputs(seed: int = 0) -> dict:
    key = jax.random.key(seed)
    ks = iter(jax.random.split(key, 48))
    f32 = jnp.float32

    def nrm(shape, scale):
        return scale * jax.random.normal(next(ks), shape, f32)

    L, C, H, N = DEPTH_2, RWKV_WIDTH, RWKV_HEADS, HEAD_SIZE
    x = nrm((BATCH, SEQ, D_MODEL), 1.0)
    c = nrm((BATCH, D_MODEL), 1.0)
    ctx = nrm((BATCH, CTX_LEN, D_MODEL), 1.0)
    c_ctx = nrm((D_MODEL,), 1.0)
    ln0_g = 1.0 + nrm((D_MODEL,), 0.05)
    ln0_b = nrm((D_MODEL,), 0.02)
    w_ada = nrm((L, D_MODEL, 6 * D_MODEL), 0.5 * D_MODEL ** -0.5)
    b_ada = nrm((L, 6 * D_MODEL), 0.02)
    w_in = nrm((L, D_MODEL, IN_WIDTH_2), D_MODEL ** -0.5)
    w_in = w_in.at[:, :, 2 * C:3 * C].multiply(DEEPNORM_BETA)
    mu_shift = jax.random.uniform(next(ks), (L, SHIFT_WIDTH), f32, 0.2, 0.8)
    w0 = jax.random.uniform(next(ks), (L, N_DIR, C), f32, -6.0, 1.0)
    w2_decay = nrm((L, N_DIR, DECAY_LORA, C), 0.5 * DECAY_LORA ** -0.5)
    a0 = nrm((L, N_DIR, C), 0.5)
    a2_iclr = nrm((L, N_DIR, ICLR_LORA, C), 0.5 * ICLR_LORA ** -0.5)
    g2_gate = nrm((L, N_DIR, GATE_LORA, C), GATE_LORA ** -0.5)
    r_k = nrm((L, N_DIR, H, N), 0.1)
    k_k = 0.85 + nrm((L, C), 0.05)
    k_a = 1.0 + nrm((L, C), 0.05)
    gn_g = 1.0 + nrm((L, C), 0.05)
    gn_b = nrm((L, C), 0.02)
    w_fno = nrm((L, FNET_GROUPS, FNET_GROUP_W, FNET_GROUP_W), FNET_GROUP_W ** -0.5)
    b_fno = nrm((L, FNET_GROUPS, FNET_GROUP_W), 0.02)
    w_out = nrm((L, MIX_WIDTH, D_MODEL), DEEPNORM_BETA * MIX_WIDTH ** -0.5)
    ln1_g = 1.0 + nrm((L, D_MODEL), 0.05)
    ln1_b = nrm((L, D_MODEL), 0.02)
    w_router = nrm((L, D_MODEL, N_EXPERTS), D_MODEL ** -0.5)
    b_router = nrm((L, N_EXPERTS), 0.01)
    w1 = nrm((L, N_EXPERTS, D_MODEL, 2 * D_FF), D_MODEL ** -0.5)
    b1 = nrm((L, N_EXPERTS, 2 * D_FF), 0.02)
    w2 = nrm((L, N_EXPERTS, D_FF, D_MODEL), DEEPNORM_BETA * D_FF ** -0.5)
    b2 = nrm((L, N_EXPERTS, D_MODEL), 0.02)
    ln2_g = 1.0 + nrm((L, D_MODEL), 0.05)
    ln2_b = nrm((L, D_MODEL), 0.02)
    return {"x": x, "c": c, "ctx": ctx, "c_ctx": c_ctx, "ln0_g": ln0_g, "ln0_b": ln0_b,
            "w_ada": w_ada, "b_ada": b_ada, "w_in": w_in, "mu_shift": mu_shift, "w0": w0,
            "w2_decay": w2_decay, "a0": a0, "a2_iclr": a2_iclr, "g2_gate": g2_gate, "r_k": r_k,
            "k_k": k_k, "k_a": k_a, "gn_g": gn_g, "gn_b": gn_b, "w_fno": w_fno, "b_fno": b_fno,
            "w_out": w_out, "ln1_g": ln1_g, "ln1_b": ln1_b, "w_router": w_router, "b_router": b_router,
            "w1": w1, "b1": b1, "w2": w2, "b2": b2, "ln2_g": ln2_g, "ln2_b": ln2_b}

def second_block(x, c, ctx, c_ctx, ln0_g, ln0_b, w_ada, b_ada, w_in, mu_shift, w0, w2_decay, a0, a2_iclr,
              g2_gate, r_k, k_k, k_a, gn_g, gn_b, w_fno, b_fno, w_out, ln1_g, ln1_b, w_router, b_router,
              w1, b1, w2, b2, ln2_g, ln2_b):
    x = layer_norm(x, ln0_g, ln0_b)
    ctx = layer_norm(ctx, ln0_g, ln0_b)
    for l in range(DEPTH_2):
        need_ctx = l < DEPTH_2 - 1
        mod = (jax.nn.silu(c) @ w_ada[l] + b_ada[l])[:, None, :]
        sh1, sc1, gt1, sh2, sc2, gt2 = jnp.split(mod, 6, axis=-1)
        mod_c = jax.nn.silu(c_ctx) @ w_ada[l] + b_ada[l]
        sh1c, sc1c, gt1c, sh2c, sc2c, gt2c = jnp.split(mod_c, 6, axis=-1)
        h = x * (1.0 + sc1) + sh1
        hc = ctx * (1.0 + sc1c) + sh1c
        mo, mo_c = token_mixer(h, hc, w_in[l], mu_shift[l], w0[l], w2_decay[l], a0[l], a2_iclr[l], g2_gate[l],
                               r_k[l], k_k[l], k_a[l], gn_g[l], gn_b[l], w_fno[l], b_fno[l], w_out[l], need_ctx)
        x = layer_norm(DEEPNORM_ALPHA * x + gt1 * mo, ln1_g[l], ln1_b[l])
        h = x * (1.0 + sc2) + sh2
        f = moe_ffn(h.reshape(-1, D_MODEL), w_router[l], b_router[l], w1[l], b1[l], w2[l], b2[l]).reshape(x.shape)
        x = layer_norm(DEEPNORM_ALPHA * x + gt2 * f, ln2_g[l], ln2_b[l])
        if need_ctx:
            ctx = layer_norm(DEEPNORM_ALPHA * ctx + gt1c * mo_c, ln1_g[l], ln1_b[l])
            hc = ctx * (1.0 + sc2c) + sh2c
            fc = moe_ffn(hc.reshape(-1, D_MODEL), w_router[l], b_router[l], w1[l], b1[l], w2[l], b2[l]).reshape(ctx.shape)
            ctx = layer_norm(DEEPNORM_ALPHA * ctx + gt2c * fc, ln2_g[l], ln2_b[l])
    return x


def setup_inputs(seed=0):
    out = dict(first_inputs(seed))
    for name, value in second_inputs(seed + 1).items():
        if name != "x":
            out[name + "_2"] = value
    return out


def reference(
    x, norm_g, w_in, b_gate, conv_dw, conv_b, conv_ln_g, conv_ln_b, ret_decay, q_norm_g,
    k_norm_g, attn_sink, w_conv_out, w_ret_out, w_attn_out, w_out, c_2, ctx_2, c_ctx_2, ln0_g_2,
    ln0_b_2, w_ada_2, b_ada_2, w_in_2, mu_shift_2, w0_2, w2_decay_2, a0_2, a2_iclr_2, g2_gate_2,
    r_k_2, k_k_2, k_a_2, gn_g_2, gn_b_2, w_fno_2, b_fno_2, w_out_2, ln1_g_2, ln1_b_2,
    w_router_2, b_router_2, w1_2, b1_2, w2_2, b2_2, ln2_g_2, ln2_b_2,
):
    x = first_block(
        x, norm_g, w_in, b_gate, conv_dw, conv_b, conv_ln_g, conv_ln_b, ret_decay, q_norm_g,
        k_norm_g, attn_sink, w_conv_out, w_ret_out, w_attn_out, w_out,
    )
    return second_block(
        x, c_2, ctx_2, c_ctx_2, ln0_g_2, ln0_b_2, w_ada_2, b_ada_2, w_in_2, mu_shift_2, w0_2,
        w2_decay_2, a0_2, a2_iclr_2, g2_gate_2, r_k_2, k_k_2, k_a_2, gn_g_2, gn_b_2, w_fno_2,
        b_fno_2, w_out_2, ln1_g_2, ln1_b_2, w_router_2, b_router_2, w1_2, b1_2, w2_2, b2_2,
        ln2_g_2, ln2_b_2,
    )


_drawn_inputs = setup_inputs


def setup_inputs(seed=0):
    import zlib

    import numpy as np

    out = dict(_drawn_inputs(seed))
    spreads = {}
    factors = {'conv_b': 4.675,
     'conv_ln_g': 6.711,
     'conv_ln_b': 8.0,
     'q_norm_g': 8.0,
     'k_norm_g': 8.0,
     'attn_sink': 8.0,
     'b_ada_2': 3.519,
     'w2_decay_2': 8.0,
     'a0_2': 3.234,
     'a2_iclr_2': 4.086,
     'r_k_2': 7.064,
     'k_k_2': 4.815,
     'k_a_2': 4.4,
     'gn_g_2': 8.0,
     'gn_b_2': 31.885,
     'b_fno_2': 27.397,
     'b_router_2': 28.086,
     'b1_2': 27.611,
     'b2_2': 8.0,
     'ln2_b_2': 2.806}
    for name, (base, spread) in spreads.items():
        noise = np.random.default_rng([zlib.crc32(name.encode()), seed]).standard_normal(out[name].shape)
        drawn = base * np.exp(spread * noise) if base else spread * noise
        out[name] = __import__('jax').numpy.asarray(drawn.astype(out[name].dtype))
    for name, factor in factors.items():
        out[name] = (out[name] * factor).astype(out[name].dtype)
    return out
```

```python
from contextlib import ExitStack

import numpy as np
import concourse.bass as bass
from concourse import mybir

ALU = mybir.AluOpType
ACT = mybir.ActivationFunctionType
F32 = mybir.dt.float32
AX_X = mybir.AxisListType.X

P = 128
D = 1024
DC = D // P
T = 256
TC = T // P
DEPTH = 2
UNIT = 512
RING = 3
EPS = 1e-6


class Signal:

    def __init__(self, ctx, nc, name, per=0, unit=1, base=0):
        self.sem = None if nc is None else ctx.enter_context(nc.semaphore(name))
        self.name, self.per, self.unit, self.base, self.n = name, per, unit, base, 0

    def at(self, turn, n):
        return self.base + n * self.unit + (0 if turn is None else turn * (self.per * self.unit))

    def now(self, turn):
        return self.at(turn, self.n)

    def one(self):
        self.n += 1
        return self.unit


def follow(before, marks, per):
    after = Signal(None, None, before.name, per, before.unit, before.base + marks * before.unit)
    after.sem = before.sem
    return after
CONST = {}
CONST_WIDTH = 0
for _name, _width in (("ones", P), ("ident", P), ("blk64", P), ("perm", P), ("dup", 2 * P), ("cosR", T), ("sinR", T),
                      ("cosA", T), ("sinA", T), ("ahead", TC * T), ("behind", TC * T), ("window", TC * T)):
    CONST[_name] = (CONST_WIDTH, CONST_WIDTH + _width)
    CONST_WIDTH += _width


def hybrid_constants():
    c = np.zeros((P, CONST_WIDTH), np.float32)

    def put(name, value):
        a, b = CONST[name]
        c[:, a:b] = np.asarray(value, np.float32).reshape(P, b - a)

    part = np.arange(P)
    pos = np.arange(T, dtype=np.float32)
    put("ones", np.ones((P, P)))
    put("ident", np.eye(P))
    put("blk64", part[:, None] // HEAD_DIM == part[None, :] // HEAD_DIM)
    half = ROPE_DIM // 2
    inside = part % HEAD_DIM
    partner = np.where(inside < half, part + half, np.where(inside < 2 * half, part - half, -1))
    put("perm", part[:, None] == partner[None, :])
    put("dup", np.stack([part[:, None] == part[None, :] % 64 + 64 * side for side in range(2)], 1))
    freq = np.float32(RET_THETA) ** (-np.arange(P, dtype=np.float32) / np.float32(P))
    ang = pos[None, :] * freq[:, None].astype(np.float32)
    put("cosR", np.cos(ang))
    put("sinR", np.sin(ang))
    freq = np.float32(ROPE_THETA) ** (-np.arange(half, dtype=np.float32) / np.float32(half))
    ang = pos[None, :] * freq[inside % half][:, None].astype(np.float32)
    turned = (inside < 2 * half)[:, None]
    put("cosA", np.where(turned, np.cos(ang), 1.0))
    put("sinA", np.where(turned, np.where(inside < half, -1.0, 1.0)[:, None] * np.sin(ang), 0.0))
    first = part[:, None] + P * np.arange(TC)[None, :]
    other = np.arange(T)[None, None, :]
    gap = other - first[:, :, None]
    put("ahead", np.maximum(gap, 0))
    put("behind", np.maximum(-gap, 0))
    put("window", np.where(np.abs(gap) <= ATTN_WINDOW, 0.0, -1e30))
    return c


HEAD_DIM = 64
ROPE_DIM = 16
ROPE_THETA = 500000.0
RET_HEADS = 4
RET_THETA = 10000.0
RET_QK = 256
RET_V = 512
ATTN_HEADS = 16
ATTN_WINDOW = 128
TAPS = 31
PAD = TAPS // 2
IN_WIDTH = 14848

PAR = {}
PAR_WIDTH = 0
for _name, _width in (("norm_g", DC), ("b_gate", 3 * DC), ("conv_b", DC), ("ln_g", DC), ("ln_b", DC),
                      ("dw", DC * TAPS), ("decay", 2 * RET_HEADS), ("qg", 1), ("kg", 1), ("sink", ATTN_HEADS)):
    PAR[_name] = PAR_WIDTH
    PAR_WIDTH += _width


def hybrid_parameters(norm_g, b_gate, conv_b, conv_ln_g, conv_ln_b, conv_dw, ret_decay, q_norm_g, k_norm_g, attn_sink):
    def down(a):
        return np.swapaxes(a.reshape(DEPTH, -1, P), 1, 2)

    def every(a):
        return np.broadcast_to(a.reshape(DEPTH, 1, -1), (DEPTH, P, a.size // DEPTH))

    taps = conv_dw.reshape(DEPTH, TAPS, DC, P).transpose(0, 3, 2, 1).reshape(DEPTH, P, DC * TAPS)
    twice = [np.concatenate([a, a], axis=1)[:, :, None] for a in (q_norm_g, k_norm_g)]
    return np.concatenate([down(norm_g), down(b_gate), down(conv_b), down(conv_ln_g), down(conv_ln_b), taps,
                           every(ret_decay), *twice, every(attn_sink)], axis=2)


Z_UNITS = IN_WIDTH // UNIT
LAYER_UNITS = Z_UNITS + 2 + 4 + 2 + 2
Z_PAIRS = 2 * Z_UNITS
Y_PAIRS = 16
PROJ_BANKS = 3
A_Q, A_KV, R_QK, R_VV, R_GATE, C_GATE, A_GATE, MIX = 18, 20, 6, 10, 14, 4, 21, 23


def hybrid_signals(ctx, nc, g):
    for name, per, *more in (
        ("x_squared", 1), ("x_sum", 1), ("x_root", 1), ("conv_root", 1), ("ret_root", 4), ("qk_root", 5), ("h_ready", 1), ("dve_step", 119), ("pool_step", 4),
        ("z_done", Z_PAIRS), ("z_out", Z_PAIRS), ("y_done", Y_PAIRS, 1, 1), ("y_out", Y_PAIRS, 1, 1),
        ("decay_sum", 1), ("decay_ready", 1), ("lambda_ready", 1),
        ("conv_tap", 8 * TAPS), ("conv_sum", 2), ("conv_centred", 1), ("conv_normed", 1), ("conv_silu", 1),
        ("conv_y", 1), ("rot_ready", 2), ("ret_scores", 4), ("ret_weighed", 4), ("ret_o", 4), ("ret_o_out", 4),
        ("ret_mean", 4), ("ret_centred", 4), ("ret_var", 4), ("ret_y", 4),
        ("qk_squared", 5), ("qk_sum", 5), ("qk_normed", 5), ("qk_swapped", 5), ("qk_ready", 5),
        ("k_twice", 2), ("k_ready", 2), ("att_scores", 16), ("att_shift", 16), ("att_exp", 16), ("att_p", 16),
        ("att_turned", 16), ("att_pt", 16), ("att_o", 16), ("att_y", 8), ("mix_ready", 3), ("merged", 1),
    ):
        g[name] = Signal(ctx, nc, name, per, *more)
    g["par_in"] = Signal(ctx, nc, "par_in", 1, 16)
    g["landed"] = [Signal(ctx, nc, f"landed{i}", LAYER_UNITS // RING, 16) for i in range(RING)]


def hybrid_memory(ctx, nc, g):
    def sb(name, shape):
        g[name] = ctx.enter_context(nc.sbuf_tensor(name, [P] + shape, F32))

    sb("par", [PAR_WIDTH])
    sb("cons", [CONST_WIDTH])
    sb("a_buf", [DC, T])
    sb("b_buf", [DC, T])
    sb("c_gate", [DC, T])
    sb("v_pad", [DC, T + 2 * PAD])
    sb("rq", [DC, T])
    sb("rk", [DC, T])
    sb("rv", [TC, 2 * D])
    sb("r_gate", [2 * DC, T])
    sb("ro", [2 * DC, T])
    sb("weighed", [2, TC, T])
    sb("aq", [DC, T])
    sb("ak", [2, T])
    sb("av", [TC, 2 * P])
    sb("decays", [RET_HEADS, TC * T])
    sb("lam", [2 * RET_HEADS])
    sb("rows", [3, T])
    sb("small", [2, 8])
    sb("pair", [2, T])
    sb("eps", [1])
    g["a_gate"] = g["v_pad"][:, :, 0:T]
    g["merged_buf"] = g["decays"][:, :, :].rearrange("p h (c t) -> p (h c) t", c=TC)
    g["ao"] = g["rq"]
    g["mix"] = [g["c_gate"][:, :, :], g["b_buf"][:, :, :],
                g["rv"][:, 0, :].rearrange("p (c t) -> p c t", t=T)]
    spent = g["r_gate"][:, 0:8, :].rearrange("p (n s c) t -> p n s c t", n=2, s=2)
    g["prob"], g["probT"] = spent[:, 0], spent[:, 1]
    g["spare"] = g["hT"]
    g["kdup"] = g["rk"][:, 0:4, :]


def hybrid_tensor(pe, nc, g, l):
    ones, blk64 = g["c"]("ones"), g["c"]("blk64")
    stat, sc, tb = [g["bank"][7][:, 0, :], g["bank"][3][:, 0, :]], [g["bank"][4], g["bank"][5]], g["bank"][6]

    def slot(u):
        s = g["landed"][u % RING]
        pe.wait_ge(s.sem, s.at(l, u // RING + 1))
        return g["ring"][:, u % RING]

    def bank_of(p):
        before = p - PROJ_BANKS
        if 0 <= before < Z_PAIRS:
            pe.wait_ge(g["z_out"].sem, g["z_out"].at(l, before + 1))
        elif before >= Z_PAIRS:
            pe.wait_ge(g["y_out"].sem, g["y_out"].at(l, before - Z_PAIRS + 1))
        return g["bank"][p % PROJ_BANKS]

    def sums(out, lhsT, rhs, n):
        for c in range(n):
            mm = nc.tensor.matmul(out, lhsT, rhs(c), start=(c == 0), stop=(c == n - 1))
        return mm

    def features(p, w, col, rhs=None, last=None):
        out = bank_of(p)
        rhs = g["hT"] if rhs is None else rhs
        for j in range(2):
            for k in range(DC):
                mm = nc.tensor.matmul(out[:, j, :], w[:, k, col + j * P:col + (j + 1) * P], rhs[:, k, :],
                                      start=(k == 0), stop=(k == DC - 1))
        return mm

    def z_unit(u):
        w = slot(u)
        features(2 * u, w, 0).then_inc(g["z_done"].sem, g["z_done"].one())
        features(2 * u + 1, w, 2 * P).then_inc(g["z_done"].sem, g["z_done"].one())

    def half_unit(p):
        w = slot(p // 2)
        features(p, w, (p % 2) * 2 * P).then_inc(g["z_done"].sem, g["z_done"].one())

    def v_unit(u):
        w = slot(u)
        for t in range(TC):
            out = bank_of(2 * u + t)
            for k in range(DC):
                mm = nc.tensor.matmul(out[:, :, :].rearrange("p a b -> p (a b)"), g["hT"][:, k, t * P:(t + 1) * P],
                                      w[:, k, :], start=(k == 0), stop=(k == DC - 1))
            mm.then_inc(g["z_done"].sem, g["z_done"].one())

    def kv_value():
        p = 2 * A_KV + 1
        w = slot(A_KV)
        out = bank_of(p)
        for t in range(TC):
            for k in range(DC):
                mm = nc.tensor.matmul(out[:, t, :], g["hT"][:, k, t * P:(t + 1) * P], w[:, k, 2 * P:4 * P],
                                      start=(k == 0), stop=(k == DC - 1))
        mm.then_inc(g["z_done"].sem, g["z_done"].one())

    pe.wait_ge(g["x_squared"].sem, g["x_squared"].at(l, 1))
    sums(stat[0], ones, lambda c: g["b_buf"][:, c, :], DC).then_inc(g["x_sum"].sem, g["x_sum"].one())
    pe.wait_ge(g["h_ready"].sem, g["h_ready"].at(l, 1))
    for u in range(R_VV):
        z_unit(u)
    for u in range(R_VV, R_GATE):
        v_unit(u)
    pe.wait_ge(g["conv_tap"].sem, g["conv_tap"].at(l, 8 * TAPS))
    sums(stat[0], ones, lambda c: g["a_buf"][:, c, :], DC).then_inc(g["conv_sum"].sem, g["conv_sum"].one())
    z_unit(R_GATE)
    z_unit(R_GATE + 1)
    pe.wait_ge(g["conv_centred"].sem, g["conv_centred"].at(l, 1))
    sums(stat[1], ones, lambda c: g["b_buf"][:, c, :], DC).then_inc(g["conv_sum"].sem, g["conv_sum"].one())
    z_unit(R_GATE + 2)
    z_unit(R_GATE + 3)

    def ret_scores(h):
        if h == 0:
            pe.wait_ge(g["rot_ready"].sem, g["rot_ready"].at(l, 2))
        else:
            pe.wait_ge(g["ret_weighed"].sem, g["ret_weighed"].at(l, h))
        out = sc[0]
        for j in range(TC):
            for d in range(2):
                mm = nc.tensor.matmul(out[:, j, :], g["rk"][:, 2 * h + d, j * P:(j + 1) * P], g["rq"][:, 2 * h + d, :],
                                      start=(d == 0), stop=(d == 1))
        mm.then_inc(g["ret_scores"].sem, g["ret_scores"].one())

    def ret_out(h):
        pe.wait_ge(g["ret_weighed"].sem, g["ret_weighed"].at(l, h + 1))
        if h:
            pe.wait_ge(g["ret_o_out"].sem, g["ret_o_out"].at(l, h))
        for v in range(4):
            for j in range(TC):
                mm = nc.tensor.matmul(g["bank"][5 + v // 2][:, v % 2, :],
                                      g["rv"][:, j, h * RET_V + v * P:h * RET_V + (v + 1) * P],
                                      g["weighed"][:, h % 2, j, :], start=(j == 0), stop=(j == TC - 1))
        mm.then_inc(g["ret_o"].sem, g["ret_o"].one())

    def ret_mean(h):
        pe.wait_ge(g["ret_o_out"].sem, g["ret_o_out"].at(l, h + 1))
        sums(stat[0], ones, lambda c: g["ro"][:, 4 * h + c, :], 4).then_inc(g["ret_mean"].sem, g["ret_mean"].one())

    def ret_var(h):
        pe.wait_ge(g["ret_centred"].sem, g["ret_centred"].at(l, h + 1))
        sums(stat[1], ones, lambda c: g["b_buf"][:, 4 * (h % 2) + c, :], 4).then_inc(
            g["ret_var"].sem, g["ret_var"].one())

    ret_scores(0)
    half_unit(36)
    ret_out(0)
    ret_scores(1)
    half_unit(37)
    ret_mean(0)
    ret_out(1)
    ret_scores(2)
    half_unit(38)
    ret_var(0)
    ret_mean(1)
    ret_out(2)
    ret_scores(3)
    half_unit(39)
    ret_var(1)
    ret_mean(2)
    ret_out(3)
    half_unit(40)
    ret_var(2)
    ret_mean(3)
    kv_value()
    ret_var(3)

    def qk_sum(n):
        pe.wait_ge(g["qk_squared"].sem, g["qk_squared"].at(l, n + 1))
        for j in range(2):
            mm = nc.tensor.matmul(sc[0][:, j, :], blk64, g["pair"][:, j, :], start=True, stop=True)
        mm.then_inc(g["qk_sum"].sem, g["qk_sum"].one())

    def qk_swap(n):
        pe.wait_ge(g["qk_normed"].sem, g["qk_normed"].at(l, n + 1))
        if n:
            pe.wait_ge(g["qk_ready"].sem, g["qk_ready"].at(l, n))
        src = g["ak"] if n == 4 else g["aq"][:, 2 * n:2 * n + 2, :]
        for j in range(2):
            mm = nc.tensor.matmul(sc[1][:, j, :], g["c"]("perm"), src[:, j, :], start=True, stop=True)
        mm.then_inc(g["qk_swapped"].sem, g["qk_swapped"].one())

    for n in range(5):
        qk_sum(n)
        half_unit(42 + n)
        qk_swap(n)
    pe.wait_ge(g["qk_ready"].sem, g["qk_ready"].at(l, 5))
    for n in range(2):
        for j in range(2):
            mm = nc.tensor.matmul([tb, sc[0]][n][:, j, :], g["c"]("dup")[:, j * P:(j + 1) * P], g["ak"][:, n, :],
                                  start=True, stop=True)
        mm.then_inc(g["k_twice"].sem, g["k_twice"].one())

    def att_scores(h):
        c, side, kv = h // 2, h % 2, h // 4
        if h == 0:
            pe.wait_ge(g["k_ready"].sem, g["k_ready"].at(l, 2))
        if h >= 2:
            pe.wait_ge(g["att_shift"].sem, g["att_shift"].at(l, h - 1))
        lo, hi = side * 64, side * 64 + 64
        for i in range(TC):
            mm = nc.tensor.matmul(sc[h % 2][:, i, :], g["aq"][lo:hi, c, i * P:(i + 1) * P], g["kdup"][lo:hi, kv, :],
                                  start=True, stop=True)
        mm.then_inc(g["att_scores"].sem, g["att_scores"].one())

    def att_turn(h):
        pe.wait_ge(g["att_p"].sem, g["att_p"].at(l, h + 1))
        if h:
            pe.wait_ge(g["att_pt"].sem, g["att_pt"].at(l, h))
        for i in range(TC):
            for j in range(TC):
                mm = nc.tensor.transpose(tb[:, j, i * P:(i + 1) * P], g["prob"][:, h % 2, i, j * P:(j + 1) * P],
                                         g["c"]("ident"))
        mm.then_inc(g["att_turned"].sem, g["att_turned"].one())

    def att_out(h):
        c, side, kv = h // 2, h % 2, h // 4
        pe.wait_ge(g["att_pt"].sem, g["att_pt"].at(l, h + 1))
        if c >= 2:
            pe.wait_ge(g["att_y"].sem, g["att_y"].at(l, c - 1))
        for j in range(TC):
            mm = nc.tensor.matmul(g["bank"][7 if c % 2 else 3][side * 64:side * 64 + 64, 0, :], g["av"][:, j, kv * 64:kv * 64 + 64],
                                  g["probT"][:, h % 2, j, :], start=(j == 0), stop=(j == TC - 1))
        mm.then_inc(g["att_o"].sem, g["att_o"].one())

    def y_pair(p, units, cols, rhs):
        ws = [slot(u) for u in units]
        out = bank_of(p)
        n = DC * len(units)
        for j in range(2):
            for k in range(n):
                mm = nc.tensor.matmul(out[:, j, :], ws[k // DC][:, k % DC, cols + j * P:cols + (j + 1) * P],
                                      rhs[:, k, :], start=(k == 0), stop=(k == n - 1))
        mm.then_inc(g["y_done"].sem, g["y_done"].one())
        return mm

    def conv_pair(i):
        if i == 0:
            pe.wait_ge(g["conv_y"].sem, g["conv_y"].at(l, 1))
        mm = y_pair(Z_PAIRS + i, [Z_UNITS + i // 2], (i % 2) * 2 * P, g["a_buf"])

    def ret_pair(i):
        if i == 0:
            pe.wait_ge(g["ret_y"].sem, g["ret_y"].at(l, 4))
        u = Z_UNITS + 2 + 2 * (i // 2)
        mm = y_pair(Z_PAIRS + 4 + i, [u, u + 1], (i % 2) * 2 * P, g["ro"])

    def fill(n):
        if 47 + n < Z_PAIRS:
            half_unit(47 + n)
        elif 47 + n < Z_PAIRS + 4:
            conv_pair(47 + n - Z_PAIRS)
        else:
            ret_pair(47 + n - Z_PAIRS - 4)

    att_scores(0)
    for h in range(ATTN_HEADS):
        if h + 1 < ATTN_HEADS:
            att_scores(h + 1)
        fill(h)
        att_turn(h)
        if h >= 1:
            att_out(h - 1)
    for n in range(ATTN_HEADS, Z_PAIRS - 47 + 8):
        fill(n)
    att_out(ATTN_HEADS - 1)
    pe.wait_ge(g["att_y"].sem, g["att_y"].at(l, 8))
    for i in range(4):
        mm = y_pair(Z_PAIRS + 8 + i, [Z_UNITS + 6 + i // 2], (i % 2) * 2 * P, g["ao"])
    pe.wait_ge(g["merged"].sem, g["merged"].at(l, 1))
    for i in range(4):
        mm = y_pair(Z_PAIRS + 12 + i, [Z_UNITS + 8 + i // 2], (i % 2) * 2 * P, g["merged_buf"])


def hybrid_scalar(act, nc, g, l):
    par = g["par"]

    def take(p, out, func):
        act.wait_ge(g["z_done"].sem, g["z_done"].at(l, p + 1))
        nc.scalar.activation(out, g["bank"][p % PROJ_BANKS][:, :, :], func).then_inc(g["z_out"].sem, g["z_out"].one())

    act.wait_ge(g["par_in"].sem, g["par_in"].at(l, 1))
    a = PAR["decay"]
    nc.scalar.activation(g["lam"][:, :], par[:, a:a + 8], ACT.Exp).then_inc(
        g["lambda_ready"].sem, g["lambda_ready"].one())

    def root(out, ssq, n, signal):
        nc.scalar.activation(out, ssq, ACT.Sqrt, bias=g["eps"][:, 0:1], scale=1.0 / n).then_inc(
            g[signal].sem, g[signal].one())

    stat, rows = [g["bank"][7][:, 0, :], g["bank"][3][:, 0, :]], g["rows"]
    act.wait_ge(g["x_sum"].sem, g["x_sum"].at(l, 1))
    root(rows[:, 0, :], stat[0], D, "x_root")
    act.wait_ge(g["decay_sum"].sem, g["decay_sum"].at(l, 1))
    nc.scalar.activation(g["decays"][:, :, :], g["decays"][:, :, :], ACT.Exp, scale=-1.0).then_inc(
        g["decay_ready"].sem, g["decay_ready"].one())
    for i in range(4):
        take(i, g["a_buf"][:, 2 * i:2 * i + 2, :], ACT.Copy)
    for i in range(4):
        take(4 + i, g["b_buf"][:, 2 * i:2 * i + 2, :], ACT.Sigmoid)
    for i in range(4):
        take(8 + i, g["c_gate"][:, 2 * i:2 * i + 2, :], ACT.Silu)
    for i in range(4):
        take(12 + i, g["rq"][:, 2 * i:2 * i + 2, :], ACT.Copy)
    for i in range(4):
        take(16 + i, g["rk"][:, 2 * i:2 * i + 2, :], ACT.Copy)
    for i in range(8):
        take(20 + i, g["rv"][:, i % 2, (i // 2) * UNIT:(i // 2 + 1) * UNIT].rearrange("p (a b) -> p a b", a=2), ACT.Copy)
    for i in range(6):
        take(28 + i, g["r_gate"][:, 2 * i:2 * i + 2, :], ACT.Silu)
    act.wait_ge(g["conv_sum"].sem, g["conv_sum"].at(l, 2))
    root(rows[:, 1, :], stat[1], D, "conv_root")
    act.wait_ge(g["conv_normed"].sem, g["conv_normed"].at(l, 1))
    for c in range(DC):
        ins = nc.scalar.activation(g["a_buf"][:, c, :], g["a_buf"][:, c, :], ACT.Silu,
                                   bias=par[:, PAR["ln_b"] + c:PAR["ln_b"] + c + 1],
                                   scale=par[:, PAR["ln_g"] + c:PAR["ln_g"] + c + 1])
    ins.then_inc(g["conv_silu"].sem, g["conv_silu"].one())
    for i in range(6, 8):
        take(28 + i, g["r_gate"][:, 2 * i:2 * i + 2, :], ACT.Silu)

    def ret_take(h):
        act.wait_ge(g["ret_o"].sem, g["ret_o"].at(l, h + 1))
        for b in range(2):
            ins = nc.scalar.activation(g["ro"][:, 4 * h + 2 * b:4 * h + 2 * b + 2, :], g["bank"][5 + b][:, :, :], ACT.Copy)
        ins.then_inc(g["ret_o_out"].sem, g["ret_o_out"].one())

    def ret_root(h):
        act.wait_ge(g["ret_var"].sem, g["ret_var"].at(l, h + 1))
        if h:
            act.wait_ge(g["ret_y"].sem, g["ret_y"].at(l, h))
        root(rows[:, 2, :], stat[1], RET_V, "ret_root")

    for h in range(4):
        take(36 + h, g["aq"][:, 2 * h:2 * h + 2, :], ACT.Copy)
        if h >= 2:
            ret_root(h - 2)
        ret_take(h)
    take(40, g["ak"][:, :, :], ACT.Copy)
    ret_root(2)
    take(41, g["av"][:, :, :], ACT.Copy)
    ret_root(3)

    def mix_take(p):
        act.wait_ge(g["z_done"].sem, g["z_done"].at(l, p + 1))
        i = 2 * (p - 2 * MIX)
        for j in range(2):
            b = PAR["b_gate"] + i + j
            ins = nc.scalar.activation(g["mix"][(i + j) // DC][:, (i + j) % DC, :], g["bank"][p % PROJ_BANKS][:, j, :],
                                       ACT.Identity, bias=par[:, b:b + 1])
        ins.then_inc(g["z_out"].sem, g["z_out"].one())

    for n in range(5):
        src = g["ak"] if n == 4 else g["aq"][:, 2 * n:2 * n + 2, :]
        if n == 0:
            act.wait_ge(g["z_out"].sem, g["z_out"].at(l, 42))
        nc.scalar.activation(g["pair"][:, :, :], src[:, :, :], ACT.Square).then_inc(
            g["qk_squared"].sem, g["qk_squared"].one())
        act.wait_ge(g["qk_sum"].sem, g["qk_sum"].at(l, n + 1))
        if n:
            act.wait_ge(g["qk_normed"].sem, g["qk_normed"].at(l, n))
        else:
            act.wait_ge(g["ret_y"].sem, g["ret_y"].at(l, 1))
        root(g["prob"][:, 0], g["bank"][4][:, :, :], HEAD_DIM, "qk_root")
        if n < 4:
            take(42 + n, g["a_gate"][:, 2 * n:2 * n + 2, :], ACT.Silu)
        else:
            mix_take(46)
    for n in range(2):
        act.wait_ge(g["k_twice"].sem, g["k_twice"].at(l, n + 1))
        if n == 0:
            act.wait_ge(g["qk_ready"].sem, g["qk_ready"].at(l, 5))
        nc.scalar.activation(g["kdup"][:, 2 * n:2 * n + 2, :], g["bank"][6 if n == 0 else 4][:, :, :], ACT.Copy).then_inc(
            
            g["k_ready"].sem, g["k_ready"].one())
    for h in range(ATTN_HEADS):
        act.wait_ge(g["att_shift"].sem, g["att_shift"].at(l, h + 1))
        s = h % 2
        for i in range(TC):
            nc.scalar.activation(g["prob"][:, s, i, :], g["prob"][:, s, i, :], ACT.Exp, bias=g["small"][:, s, i:i + 1],
                                 accum_out=g["small"][:, s, 4 + i:5 + i])
        nc.scalar.activation(g["small"][:, s, 2:4], g["small"][:, s, 2:4], ACT.Exp).then_inc(
            g["att_exp"].sem, g["att_exp"].one())
        if 47 + h < Z_PAIRS:
            mix_take(47 + h)
        act.wait_ge(g["att_turned"].sem, g["att_turned"].at(l, h + 1))
        if h >= 2:
            act.wait_ge(g["att_o"].sem, g["att_o"].at(l, h - 1))
        nc.scalar.activation(g["probT"][:, s], g["bank"][6][:, :, :], ACT.Copy).then_inc(
            g["att_pt"].sem, g["att_pt"].one())
        if h == 11:
            act.wait_ge(g["z_out"].sem, g["z_out"].at(l, Z_PAIRS))
            for b in range(3):
                nc.scalar.activation(g["mix"][b], g["mix"][b], ACT.Sigmoid).then_inc(
                    g["mix_ready"].sem, g["mix_ready"].one())


def hybrid_pool(pool, nc, g, l):
    step = g["pool_step"]

    pool.wait_ge(g["y_out"].sem, g["y_out"].at(l, 0))
    pool.dma_start(g["par"][:, :], g["par_dram"][bass.ds(l, 1), :, :].rearrange("o p n -> (o p) n")).then_inc(
        g["par_in"].sem, g["par_in"].one())
    cos, sin = (g["c"](n).unsqueeze(1).to_broadcast([P, RET_HEADS, T]) for n in ("cosR", "sinR"))
    s1, s2 = (g["ro"][:, 4 * i:4 * i + 4, :] for i in range(2))
    for n, name in enumerate(("rq", "rk")):
        both = g[name][:, :, :].rearrange("p (h s) t -> p h s t", s=2)
        x1, x2 = both[:, :, 0, :], both[:, :, 1, :]
        pool.wait_ge(g["z_out"].sem, g["z_out"].at(l, 16 + 4 * n))
        nc.gpsimd.tensor_tensor(s1, x2, sin, ALU.mult)
        nc.gpsimd.tensor_tensor(s2, x1, sin, ALU.mult).then_inc(g["pool_step"].sem, g["pool_step"].one())
        pool.wait_ge(g["pool_step"].sem, g["pool_step"].now(l))
        nc.gpsimd.tensor_tensor(x1, x1, cos, ALU.mult)
        nc.gpsimd.tensor_tensor(x2, x2, cos, ALU.mult).then_inc(g["pool_step"].sem, g["pool_step"].one())
        pool.wait_ge(g["pool_step"].sem, g["pool_step"].now(l))
        nc.gpsimd.tensor_tensor(x1, x1, s1, ALU.subtract)
        ins = nc.gpsimd.tensor_tensor(x2, x2, s2, ALU.add)
        ins.then_inc(g["rot_ready"].sem, g["rot_ready"].one())
        if n == 0:
            pool.wait_ge(g["rot_ready"].sem, g["rot_ready"].at(l, 1))


def hybrid_vector(dve, nc, g, l):
    par, step, rows, sm = g["par"], g["dve_step"], g["rows"], g["small"]
    stat = [g["bank"][7][:, 0, :], g["bank"][3][:, 0, :]]

    def over(row, n):
        return row.unsqueeze(1).to_broadcast([P, n, T])

    def inverse(row, root, n):
        dve.wait_ge(g[root].sem, g[root].at(l, n))
        nc.vector.reciprocal(row, row).then_inc(g["dve_step"].sem, g["dve_step"].one())
        dve.wait_ge(g["dve_step"].sem, g["dve_step"].now(l))

    xT, hT = g["xT"], g["hT"]
    nc.vector.tensor_tensor(g["b_buf"][:, :, :], xT[:, :, :], xT[:, :, :], ALU.mult).then_inc(
        g["x_squared"].sem, g["x_squared"].one())
    inverse(rows[:, 0, :], "x_root", 1)
    dve.wait_ge(g["par_in"].sem, g["par_in"].at(l, 1))
    for c in range(DC):
        ins = nc.vector.scalar_tensor_tensor(out=hT[:, c, :], in0=xT[:, c, :],
                                             scalar=par[:, PAR["norm_g"] + c:PAR["norm_g"] + c + 1],
                                             in1=rows[:, 0, :], op0=ALU.mult, op1=ALU.mult)
    ins.then_inc(g["h_ready"].sem, g["h_ready"].one())
    dve.wait_ge(g["lambda_ready"].sem, g["lambda_ready"].at(l, 1))
    dec = g["decays"]
    for h in range(RET_HEADS):
        ins = nc.vector.tensor_scalar(dec[:, h, :], g["c"]("ahead"), g["lam"][:, h:h + 1], None, ALU.mult)
    ins.then_inc(g["dve_step"].sem, g["dve_step"].one())
    dve.wait_ge(g["dve_step"].sem, g["dve_step"].now(l))
    for h in range(RET_HEADS):
        ins = nc.vector.scalar_tensor_tensor(out=dec[:, h, :], in0=g["c"]("behind"), scalar=g["lam"][:, 4 + h:5 + h],
                                             in1=dec[:, h, :], op0=ALU.mult, op1=ALU.add)
    ins.then_inc(g["decay_sum"].sem, g["decay_sum"].one())
    dve.wait_ge(g["z_out"].sem, g["z_out"].at(l, 8))
    v, y = g["v_pad"], g["a_buf"]
    nc.vector.memset(v[:, :, 0:PAD], 0.0)
    nc.vector.memset(v[:, :, PAD + T:T + 2 * PAD], 0.0)
    nc.vector.tensor_tensor(v[:, :, PAD:PAD + T], g["a_buf"][:, :, :], g["b_buf"][:, :, :], ALU.mult).then_inc(
        g["dve_step"].sem, g["dve_step"].one())
    dve.wait_ge(g["dve_step"].sem, g["dve_step"].now(l))
    for t in range(TAPS):
        for c in range(DC):
            w = par[:, PAR["dw"] + c * TAPS + t:PAR["dw"] + c * TAPS + t + 1]
            if t == 0:
                ins = nc.vector.tensor_scalar(y[:, c, :], v[:, c, 0:T], w, par[:, PAR["conv_b"] + c:PAR["conv_b"] + c + 1],
                                              ALU.mult, ALU.add)
            else:
                dve.wait_ge(g["conv_tap"].sem, g["conv_tap"].at(l, t * DC + c - 7))
                ins = nc.vector.scalar_tensor_tensor(out=y[:, c, :], in0=v[:, c, t:t + T], scalar=w, in1=y[:, c, :],
                                                     op0=ALU.mult, op1=ALU.add)
            ins.then_inc(g["conv_tap"].sem, g["conv_tap"].one())
    dve.wait_ge(g["conv_sum"].sem, g["conv_sum"].at(l, 1))
    nc.vector.tensor_scalar(rows[:, 0, :], stat[0], 1.0 / D, None, ALU.mult).then_inc(
        g["dve_step"].sem, g["dve_step"].one())
    dve.wait_ge(g["dve_step"].sem, g["dve_step"].now(l))
    nc.vector.tensor_tensor(y[:, :, :], y[:, :, :], over(rows[:, 0, :], DC), ALU.subtract).then_inc(
        g["dve_step"].sem, g["dve_step"].one())
    dve.wait_ge(g["dve_step"].sem, g["dve_step"].now(l))
    nc.vector.tensor_tensor(g["b_buf"][:, :, :], y[:, :, :], y[:, :, :], ALU.mult).then_inc(
        g["conv_centred"].sem, g["conv_centred"].one())
    inverse(rows[:, 1, :], "conv_root", 1)
    nc.vector.tensor_tensor(y[:, :, :], y[:, :, :], over(rows[:, 1, :], DC), ALU.mult).then_inc(
        g["conv_normed"].sem, g["conv_normed"].one())

    def ret_weigh(h):
        dve.wait_ge(g["ret_scores"].sem, g["ret_scores"].at(l, h + 1))
        if h == 0:
            dve.wait_ge(g["decay_ready"].sem, g["decay_ready"].at(l, 1))
        if h >= 2:
            dve.wait_ge(g["ret_o"].sem, g["ret_o"].at(l, h - 1))
        nc.vector.scalar_tensor_tensor(out=g["weighed"][:, h % 2].rearrange("p a b -> p (a b)"),
                                       in0=g["bank"][4][:, :, :].rearrange("p a b -> p (a b)"),
                                       scalar=float(RET_QK) ** -0.5, in1=dec[:, h, :], op0=ALU.mult, op1=ALU.mult).then_inc(
                                           
            g["ret_weighed"].sem, g["ret_weighed"].one())

    def ret_centre(h):
        dve.wait_ge(g["ret_mean"].sem, g["ret_mean"].at(l, h + 1))
        o = g["ro"][:, 4 * h:4 * h + 4, :]
        nc.vector.tensor_scalar(rows[:, 0, :], stat[0], 1.0 / RET_V, None, ALU.mult).then_inc(
            g["dve_step"].sem, g["dve_step"].one())
        dve.wait_ge(g["dve_step"].sem, g["dve_step"].now(l))
        nc.vector.tensor_tensor(o, o, over(rows[:, 0, :], 4), ALU.subtract).then_inc(
            g["dve_step"].sem, g["dve_step"].one())
        dve.wait_ge(g["dve_step"].sem, g["dve_step"].now(l))
        nc.vector.tensor_tensor(g["b_buf"][:, 4 * (h % 2):4 * (h % 2) + 4, :], o, o, ALU.mult).then_inc(
            g["ret_centred"].sem, g["ret_centred"].one())

    def ret_norm(h):
        o = g["ro"][:, 4 * h:4 * h + 4, :]
        inverse(rows[:, 2, :], "ret_root", h + 1)
        nc.vector.tensor_tensor(o, o, over(rows[:, 2, :], 4), ALU.mult).then_inc(g["dve_step"].sem, g["dve_step"].one())
        dve.wait_ge(g["dve_step"].sem, g["dve_step"].now(l))
        nc.vector.tensor_tensor(o, o, g["r_gate"][:, 4 * h:4 * h + 4, :], ALU.mult).then_inc(
            g["ret_y"].sem, g["ret_y"].one())

    ret_weigh(0)
    dve.wait_ge(g["conv_silu"].sem, g["conv_silu"].at(l, 1))
    nc.vector.tensor_tensor(y[:, :, :], y[:, :, :], g["c_gate"][:, :, :], ALU.mult).then_inc(
        g["conv_y"].sem, g["conv_y"].one())
    ret_weigh(1)
    ret_centre(0)
    ret_weigh(2)
    ret_norm(0)
    ret_centre(1)
    ret_weigh(3)
    ret_norm(1)
    ret_centre(2)
    ret_norm(2)
    ret_centre(3)
    ret_norm(3)

    for n in range(5):
        src = g["ak"][:, :, :] if n == 4 else g["aq"][:, 2 * n:2 * n + 2, :]
        two = g["prob"][:, 0]
        turned = g["prob"][:, 1]
        inverse(two, "qk_root", n + 1)
        gain = PAR["kg" if n == 4 else "qg"]
        nc.vector.scalar_tensor_tensor(out=src, in0=src, scalar=par[:, gain:gain + 1], in1=two,
                                       op0=ALU.mult, op1=ALU.mult).then_inc(g["qk_normed"].sem, g["qk_normed"].one())
        dve.wait_ge(g["qk_swapped"].sem, g["qk_swapped"].at(l, n + 1))
        nc.vector.tensor_tensor(turned, g["bank"][5][:, :, :], over(g["c"]("sinA"), 2), ALU.mult)
        nc.vector.tensor_tensor(src, src, over(g["c"]("cosA"), 2), ALU.mult).then_inc(
            g["dve_step"].sem, g["dve_step"].one())
        dve.wait_ge(g["dve_step"].sem, g["dve_step"].now(l))
        nc.vector.tensor_tensor(src, src, turned, ALU.add).then_inc(g["qk_ready"].sem, g["qk_ready"].one())

    def att_shift(h):
        dve.wait_ge(g["att_scores"].sem, g["att_scores"].at(l, h + 1))
        s = h % 2
        if h >= 2:
            dve.wait_ge(g["att_turned"].sem, g["att_turned"].at(l, h - 1))
        if h == 0:
            dve.wait_ge(g["qk_ready"].sem, g["qk_ready"].at(l, 5))
        sink = par[:, PAR["sink"] + h:PAR["sink"] + h + 1]
        nc.vector.scalar_tensor_tensor(out=g["prob"][:, s].rearrange("p a b -> p (a b)"),
                                       in0=g["bank"][4 + s][:, :, :].rearrange("p a b -> p (a b)"),
                                       scalar=float(HEAD_DIM) ** -0.5, in1=g["c"]("window"),
                                       op0=ALU.mult, op1=ALU.add).then_inc(g["dve_step"].sem, g["dve_step"].one())
        dve.wait_ge(g["dve_step"].sem, g["dve_step"].now(l))
        nc.vector.tensor_reduce(sm[:, s, 6:8], g["prob"][:, s], AX_X, ALU.max).then_inc(
            g["dve_step"].sem, g["dve_step"].one())
        dve.wait_ge(g["dve_step"].sem, g["dve_step"].now(l))
        nc.vector.tensor_scalar(sm[:, s, 0:2], sm[:, s, 6:8], sink, -1.0, ALU.max, ALU.mult).then_inc(
            g["dve_step"].sem, g["dve_step"].one())
        dve.wait_ge(g["dve_step"].sem, g["dve_step"].now(l))
        nc.vector.tensor_scalar(sm[:, s, 2:4], sm[:, s, 0:2], sink, None, ALU.add).then_inc(
            g["att_shift"].sem, g["att_shift"].one())

    def att_norm(h):
        dve.wait_ge(g["att_exp"].sem, g["att_exp"].at(l, h + 1))
        s = h % 2
        nc.vector.tensor_tensor(sm[:, s, 4:6], sm[:, s, 4:6], sm[:, s, 2:4], ALU.add).then_inc(
            g["dve_step"].sem, g["dve_step"].one())
        dve.wait_ge(g["dve_step"].sem, g["dve_step"].now(l))
        nc.vector.reciprocal(sm[:, s, 4:6], sm[:, s, 4:6]).then_inc(g["dve_step"].sem, g["dve_step"].one())
        dve.wait_ge(g["dve_step"].sem, g["dve_step"].now(l))
        for i in range(TC):
            ins = nc.vector.tensor_scalar(g["prob"][:, s, i, :], g["prob"][:, s, i, :], sm[:, s, 4 + i:5 + i], None, ALU.mult)
        ins.then_inc(g["att_p"].sem, g["att_p"].one())

    def att_gate(c):
        dve.wait_ge(g["att_o"].sem, g["att_o"].at(l, 2 * c + 2))
        nc.vector.tensor_tensor(g["ao"][:, c, :], stat[(c + 1) % 2], g["a_gate"][:, c, :], ALU.mult).then_inc(
            g["att_y"].sem, g["att_y"].one())

    merged = g["merged_buf"]
    spare = g["spare"]

    def y_take(i, b):
        dve.wait_ge(g["y_done"].sem, g["y_done"].at(l, 4 * b + i + 1))
        bank = g["bank"][(Z_PAIRS + 4 * b + i) % PROJ_BANKS][:, :, :]
        if b == 0:
            nc.vector.tensor_tensor(merged[:, 2 * i:2 * i + 2, :], bank, g["mix"][0][:, 2 * i:2 * i + 2, :], ALU.mult).then_inc(
                
                g["y_out"].sem, g["y_out"].one())
            return
        nc.vector.tensor_tensor(spare[:, 2 * i:2 * i + 2, :], bank, g["mix"][b][:, 2 * i:2 * i + 2, :], ALU.mult).then_inc(
            
            g["y_out"].sem, g["y_out"].one())
        dve.wait_ge(g["y_out"].sem, g["y_out"].at(l, 4 * b + i + 1))
        ins = nc.vector.tensor_tensor(merged[:, 2 * i:2 * i + 2, :], merged[:, 2 * i:2 * i + 2, :],
                                      spare[:, 2 * i:2 * i + 2, :], ALU.add)
        if b == 2 and i == 3:
            ins.then_inc(g["merged"].sem, g["merged"].one())
        else:
            ins.then_inc(g["dve_step"].sem, g["dve_step"].one())
            dve.wait_ge(g["dve_step"].sem, g["dve_step"].now(l))

    att_shift(0)
    att_shift(1)
    for h in range(ATTN_HEADS):
        att_norm(h)
        if h == ATTN_HEADS - 2:
            dve.wait_ge(g["mix_ready"].sem, g["mix_ready"].at(l, 3))
        if h >= ATTN_HEADS - 2:
            for i in range(2):
                y_take(2 * (h - ATTN_HEADS + 2) + i, 0)
        if h >= 2 and h % 2 == 0:
            att_gate(h // 2 - 1)
        if h + 2 < ATTN_HEADS:
            att_shift(h + 2)
    for i in range(4):
        y_take(i, 1)
    att_gate(7)
    for i in range(4):
        y_take(i, 2)
    for i in range(4):
        dve.wait_ge(g["y_done"].sem, g["y_done"].at(l, 12 + i + 1))
        nc.vector.tensor_tensor(xT[:, 2 * i:2 * i + 2, :], xT[:, 2 * i:2 * i + 2, :],
                                g["bank"][(Z_PAIRS + 12 + i) % PROJ_BANKS][:, :, :], ALU.add).then_inc(
            g["y_out"].sem, g["y_out"].one())
    dve.wait_ge(g["y_out"].sem, g["y_out"].at(l, Y_PAIRS))


def hybrid_loads(sp, nc, g, l):
    for u in range(LAYER_UNITS):
        v = u - RING
        if v < 0:
            sp.wait_ge(g["y_done"].sem, 1 + l * (Y_PAIRS - 2 * (-1 - v)))
        elif v < Z_UNITS:
            sp.wait_ge(g["z_done"].sem, g["z_done"].at(l, 2 * (v + 1)))
        else:
            sp.wait_ge(g["y_done"].sem, g["y_done"].at(l, OUT_Y[v - Z_UNITS]))
        if u < Z_UNITS:
            src = g["w_in"][bass.ds(l, 1), :, u * UNIT:(u + 1) * UNIT]
        else:
            name, i = next((n, u - Z_UNITS - a) for n, a, b in OUT_UNITS if a <= u - Z_UNITS < b)
            row, col = (D * (i % 2), UNIT * (i // 2)) if name == "w_ret_out" else (0, UNIT * i)
            src = g[name][bass.ds(l, 1), row:row + D, col:col + UNIT]
        sp.dma_start(g["ring"][:, u % RING], src.rearrange("o (k p) n -> p (o k) n", p=P)).then_inc(
            g["landed"][u % RING].sem, g["landed"][u % RING].one())


OUT_Y = (2, 4, 6, 6, 8, 8, 10, 12, 14, 16)
OUT_UNITS = (("w_conv_out", 0, 2), ("w_ret_out", 2, 6), ("w_attn_out", 6, 8), ("w_out", 8, 10))


C2 = 64
NC = 4
DIRS = 2
DN = DIRS * NC
SHIFTED = 16
STEPS = T // C2
LEVELS = 5
GRID_W = 64
GRID_H = T // GRID_W
ADA_UNITS, IN_UNITS, MO_UNITS = 12, 5, 2
B_UNITS = ADA_UNITS + IN_UNITS + MO_UNITS
LN_EPS, GN_EPS = 1e-5, 64e-5
ALPHA = 2.0 ** 0.25
LOG_W = -float(np.exp(-0.5))
SH1, SC1, GT1, SH2, SC2, GT2 = (DC * i for i in range(6))

MIX_CONST = {}
MIX_CONST_WIDTH = 0
for _name, _width in (("reset", 2 * T), ("keep", DIRS * 2 * C2), ("first", DIRS * C2), ("eye", C2),
                      ("levels", LEVELS * DIRS * C2), ("chan", 2 * P), ("timeC", TC * T), ("timeS", TC * T)):
    MIX_CONST[_name] = (MIX_CONST_WIDTH, MIX_CONST_WIDTH + _width)
    MIX_CONST_WIDTH += _width


def mixer_constants():
    c = np.zeros((P, MIX_CONST_WIDTH), np.float32)

    def put(name, value):
        a, b = MIX_CONST[name]
        c[:, a:b] = np.asarray(value, np.float64).reshape(P, b - a)

    s = (np.arange(P) % C2)[:, None]
    t = np.arange(C2)[None, :]
    put("reset", np.broadcast_to(np.arange(2 * T) % C2 != 0, (P, 2 * T)))
    put("keep", np.stack([s < t, s <= t, s > t, s >= t], 1))

    def level(size, row, col):
        return (row // (2 * size) == col // (2 * size)) & (row // size % 2 == 1) & (col // size % 2 == 0)

    put("first", np.stack([level(1, s, t), level(1, t, s)], 1))
    put("eye", s == t)
    put("levels", np.stack([np.stack([level(2 ** k, t, s), level(2 ** k, s, t)], 1) for k in range(1, LEVELS + 1)], 1))
    part = np.arange(P)
    same = part[:, None] // 64 == part[None, :] // 64
    turn = 2 * np.pi * ((part[:, None] % 64) * (part[None, :] % 64) % 64) / 64
    put("chan", np.concatenate([np.cos(turn) * same / 8, np.sin(turn) * same / 8], 1))
    token = part[:, None] + P * np.arange(TC)[None, :]
    turn = 2 * np.pi * (token[:, :, None] * np.arange(T)[None, None, :] % T) / T
    put("timeC", np.cos(turn) / 16)
    put("timeS", -np.sin(turn) / 16)
    return c


MIX_PAR = {}
MIX_PAR_WIDTH = 0
for _name, _width in (("ln0_g", DC), ("ln0_b", DC), ("b_ada", 6 * DC), ("mu", SHIFTED), ("w0", DN), ("a0", DN),
                      ("r_k", DN), ("k_k", NC), ("k_a", NC), ("gn_g", NC), ("gn_b", NC), ("b_fno", NC),
                      ("ln1_g", DC), ("ln1_b", DC), ("ln2_g", DC), ("ln2_b", DC), ("cond", 2 * DC)):
    MIX_PAR[_name] = MIX_PAR_WIDTH
    MIX_PAR_WIDTH += _width


def mixer_parameters(ln0_g, ln0_b, b_ada, mu_shift, w0, a0, r_k, k_k, k_a, gn_g, gn_b, b_fno, ln1_g, ln1_b, ln2_g, ln2_b,
                     c, c_ctx):
    rows = [a.reshape(-1, P).T for a in (ln0_g, ln0_b, b_ada, mu_shift, w0, a0, r_k, k_k, k_a, gn_g, gn_b, b_fno,
                                         ln1_g, ln1_b, ln2_g, ln2_b)]
    cond = np.stack([c.reshape(-1, P).T, c_ctx.reshape(-1, P).T], axis=2).reshape(P, 2 * DC)
    return np.concatenate(rows + [cond], axis=1)


def mixer_signals(ctx, nc, g):
    for name, per, *more in (
        ("ada_unit", ADA_UNITS), ("row_out", ADA_UNITS), ("mod_turned", 1), ("cond_ready", 1), ("stack_ready", 1),
        ("ln_sum", 4), ("ln_centred", 1), ("ln_root", 2), ("h2_ready", 1), ("p_done", 20),
        ("p_out", 20), ("shifted", 4), ("gates_ready", 2), ("lora_done", 16), ("lora_out", 16),
        ("g_done", 8), ("g_out", 8), ("kk_squared", 1), ("kk_sum", 4), ("kk_root", 4), ("decay_set", 1), ("exps_ready", 2),
        ("staged", 1), ("state_ready", 1, 1, 1), ("tok_done", 3), ("tok_out", 3), ("pairs_done", 4), ("pairs_out", 4),
        ("first_done", 1), ("x_ready", 1), ("levels_cut", LEVELS), ("t_done", 2 * LEVELS), ("t_out", 2 * LEVELS),
        ("d_done", 2 * LEVELS), ("x_next", 2 * LEVELS), ("g0_done", 1), ("g0_out", 1), ("u_done", 2),
        ("u_out", 2), ("y_step", 2), ("y_kept", 1, 1, 1), ("s_done", 2), ("ctx_dve", 2), ("lat_dve", 2),
        ("gn_sum", 8), ("gn_centred", 1), ("gn_root", 4), ("bonus_ready", 1), ("bonus_sum", 4),
        ("bonus_out", 4), ("cat_ready", 1), ("f_a", 4), ("f_a_out", 4), ("f_b", 2), ("f_b_out", 2), ("f_c", 2), ("f_c_out", 2),
        ("mo_done", 4), ("mo_out", 4), ("res_squared", 1),
    ):
        g[name] = Signal(ctx, nc, name, per, *more)
    g["mix_in"] = Signal(ctx, nc, "mix_dma", 7, 16)


def mixer_memory(ctx, nc, g):
    def sb(name, shape):
        g[name] = ctx.enter_context(nc.sbuf_tensor(name, [P] + shape, F32))
        return g[name]

    sb("mcons", [MIX_CONST_WIDTH])
    g["mc"] = lambda name: g["mcons"][:, MIX_CONST[name][0]:MIX_CONST[name][1]]
    sb("w2d", [NC * P])
    sb("a2i", [NC * P])
    sb("g2g", [DIRS, NC * P])
    sb("wf", [NC, P])
    sb("stack", [DC, 2 * T])
    sb("squares", [DC, 2 * T])
    lat, con, near = NC * (GRID_H + 2) * (GRID_W + 2), NC * (T + 2), 2 * NC * T
    shift = sb("shift", [lat + con + near])
    g["lat_pad"] = shift[:, 0:lat].rearrange("p (n a b) -> p n a b", n=NC, a=GRID_H + 2)
    g["ctx_pad"] = shift[:, lat:lat + con].rearrange("p (n t) -> p n t", n=NC)
    g["near"] = shift[:, lat + con:lat + con + near].rearrange("p (s n t) -> p s n t", s=2, n=NC)
    g["grow"] = shift[:, 0:DN * T].rearrange("p (n t) -> p n t", n=DN)
    g["yy"] = shift[:, DN * T:2 * DN * T].rearrange("p (n t) -> p n t", n=DN)
    sb("m_r", [NC, T])
    sb("m_k", [NC, 2 * T])
    sb("m_v", [NC, 2 * T])
    sb("m_wag", [4, 2 * T])
    sb("m_f", [NC, T])
    early = sb("early", [2 * DN, 2 * T])
    g["iclr"], g["kd"] = early[:, 0:DN, :], early[:, DN:2 * DN, :]
    sb("kk", [NC, 2 * T])
    sb("total", [DN, 2 * STEPS])
    sb("eps2", [3])
    flat = g["ring"][:, :, :, :].rearrange("p a b c -> p (a b c)")
    at = 0
    for name, width in (("sA", 2), ("sB", 1), ("sK", 1), ("sV", 1), ("tB", 1), ("tK", 1), ("tV", 1), ("MP", 2), ("NQ", 2),
                        ("XX", 2), ("T1", 1), ("G0", 1), ("U", 1), ("sum", 1),
                        ("ST", 1)):
        w = width * DN * C2
        g[name] = flat[:, at:at + w].rearrange("p (n w) -> p n w", n=DN)
        at += w
    g["XX"] = g["XX"].rearrange("p n w -> p (n w)").rearrange("p (d s c w) -> p d s c w", d=DIRS, s=2, c=NC)
    g["cut"] = flat[:, at:at + LEVELS * DN * C2].rearrange("p (k n w) -> p k n w", k=LEVELS, n=DN)


def row(ap, n):
    return ap.unsqueeze(1).to_broadcast([P, n, ap.shape[-1]])


def mixer_loads(sp, nc, g):
    for u in range(ADA_UNITS + IN_UNITS):
        v = u - RING
        if v >= ADA_UNITS:
            sp.wait_ge(g["p_done"].sem, g["p_done"].at(None, 4 * (v - ADA_UNITS + 1)))
        elif v >= 0:
            sp.wait_ge(g["ada_unit"].sem, g["ada_unit"].at(None, v + 1))
        else:
            sp.wait_ge(g["y_done"].sem, g["y_done"].at(DEPTH - 1, OUT_Y[len(OUT_Y) - RING + u]))
        src = g["w_ada"][0, :, u * UNIT:(u + 1) * UNIT] if u < ADA_UNITS else \
            g["w_in2"][0, :, (u - ADA_UNITS) * UNIT:(u - ADA_UNITS + 1) * UNIT]
        sp.dma_start(g["ring"][:, u % RING], src.rearrange("(k p) n -> p k n", p=P)).then_inc(
            g["landed_b"][u % RING].sem, g["landed_b"][u % RING].one())
    sp.wait_ge(g["staged"].sem, g["staged"].at(2 * STEPS - 1, 3))
    sp.wait_ge(g["state_ready"].sem, g["state_ready"].at(2 * STEPS - 1, 1))
    sp.wait_ge(g["y_kept"].sem, g["y_kept"].at(STEPS - 1, 1))
    for i in range(MO_UNITS):
        u = ADA_UNITS + IN_UNITS + i
        sp.dma_start(g["ring"][:, u % RING], g["w_out2"][0, :, i * UNIT:(i + 1) * UNIT].rearrange("(k p) n -> p k n", p=P)).then_inc(
            
            g["landed_b"][u % RING].sem, g["landed_b"][u % RING].one())


def chunk_start(lat, i, d):
    base = T if lat else 0
    return base + (i * C2 if d == 0 else (STEPS - 1) * C2 - i * C2)


def mixer_pool(pool, nc, g, moe):
    pool.wait_ge(g["y_out"].sem, g["y_out"].at(None, DEPTH * Y_PAIRS))
    nc.gpsimd.memset(g["wf"][:, :, :], 0.0).then_inc(g["wf_zero"].sem, g["wf_zero"].one())
    pool.wait_ge(g["wf_zero"].sem, 1)
    pool.dma_start(g["stack"][:, :, 0:T], g["ctxT"]).then_inc(g["mix_in"].sem, g["mix_in"].one())
    pool.dma_start(g["mcons"][:, :], g["mcons_dram"]).then_inc(g["mix_in"].sem, g["mix_in"].one())
    pool.dma_start(g["w2d"][:, :], g["w2_decay"][0].rearrange("d r c -> (d r) c")).then_inc(
        g["mix_in"].sem, g["mix_in"].one())
    pool.dma_start(g["a2i"][:, :], g["a2_iclr"][0].rearrange("d r c -> (d r) c")).then_inc(
        g["mix_in"].sem, g["mix_in"].one())
    pool.dma_start(g["g2g"][:, :, :], g["g2_gate"][0].rearrange("d r c -> r d c")).then_inc(
        g["mix_in"].sem, g["mix_in"].one())
    for side in range(2):
        lo, hi = side * 64, side * 64 + 64
        pool.dma_start(g["wf"][lo:hi, :, lo:hi], g["w_fno"][0, side::2].rearrange("g c e -> c g e")).then_inc(
            g["mix_in"].sem, g["mix_in"].one())

    moe_early_loads(pool, nc, moe)

    def cuts(turn):
        pool.wait_ge(g["pairs_out"].sem, g["pairs_out"].at(turn, 2))
        for k in range(LEVELS):
            mask = g["mc"]("levels").rearrange("p (k d t) -> p k d t", k=LEVELS, d=DIRS)
            for d in range(DIRS):
                ins = nc.gpsimd.tensor_tensor(g["cut"][:, k, d * NC:(d + 1) * NC, :], g["MP"][:, d * NC:(d + 1) * NC, 0:C2],
                                              row(mask[:, k, d, :], NC), ALU.mult)
            ins.then_inc(g["levels_cut"].sem, g["levels_cut"].one())

    with pool.Fori(0, STEPS) as i:
        cuts(i)
    g["levels_cut"].n = 0
    with pool.Fori(0, STEPS) as i:
        cuts(i + STEPS)


def mixer_tensor(pe, nc, g):
    ones, blk64 = g["c"]("ones"), g["c"]("blk64")
    flat = [b[:, :, :].rearrange("p a b -> p (a b)") for b in g["bank"]]

    def slot(u):
        s = g["landed_b"][u % RING]
        pe.wait_ge(s.sem, s.at(None, u // RING + 1))
        return g["ring"][:, u % RING]

    pe.wait_ge(g["cond_ready"].sem, g["cond_ready"].at(None, 1))
    pe.wait_ge(g["y_out"].sem, g["y_out"].at(None, DEPTH * Y_PAIRS))

    def turn_rows(u):
        pe.wait_ge(g["row_out"].sem, g["row_out"].at(None, u + 1))
        for n in range(4 * u, 4 * u + 4):
            mm = nc.tensor.matmul(flat[4][:, 2 * n:2 * n + 2], g["rows"][0:2, n * P:(n + 1) * P], g["c"]("ident")[0:2, 0:2],
                                  start=True, stop=True)
        return mm

    for u in range(ADA_UNITS):
        w = slot(u)
        if u >= 2:
            pe.wait_ge(g["row_out"].sem, g["row_out"].at(None, u - 1))
        for k in range(DC):
            mm = nc.tensor.matmul(flat[5 + u % 2][0:2, :], g["cond"][:, k, :], w[:, k, :], start=(k == 0), stop=(k == DC - 1))
        mm.then_inc(g["ada_unit"].sem, g["ada_unit"].one())
        if u:
            turn_rows(u - 1)
        if u == 2:
            pe.wait_ge(g["stack_ready"].sem, g["stack_ready"].at(None, 1))
            for c in range(DC):
                mm = nc.tensor.matmul(flat[1], ones, g["stack"][:, c, :], start=(c == 0), stop=(c == DC - 1))
            mm.then_inc(g["ln_sum"].sem, g["ln_sum"].one())
        if u == 5:
            pe.wait_ge(g["ln_centred"].sem, g["ln_centred"].at(None, 1))
            for c in range(DC):
                mm = nc.tensor.matmul(flat[2], ones, g["squares"][:, c, :], start=(c == 0), stop=(c == DC - 1))
            mm.then_inc(g["ln_sum"].sem, g["ln_sum"].one())
    turn_rows(ADA_UNITS - 1).then_inc(g["mod_turned"].sem, g["mod_turned"].one())
    pe.wait_ge(g["h2_ready"].sem, g["h2_ready"].at(None, 1))
    for u in range(IN_UNITS):
        w = slot(ADA_UNITS + u)
        for j in range(4):
            q = 4 * u + j
            if q >= 4:
                pe.wait_ge(g["p_out"].sem, g["p_out"].at(None, q - 3))
            lo = T if latent_only(q) else 0
            for k in range(DC):
                mm = nc.tensor.matmul(flat[q % 4][:, 0:2 * T - lo], w[:, k, j * P:(j + 1) * P], g["stack"][:, k, lo:2 * T],
                                      start=(k == 0), stop=(k == DC - 1))
            mm.then_inc(g["p_done"].sem, g["p_done"].one())
    pe.wait_ge(g["kk_squared"].sem, g["kk_squared"].at(None, 1))
    for c in range(NC):
        nc.tensor.matmul(flat[4 + c], blk64, g["squares"][:, c, :], start=True, stop=True).then_inc(
            g["kk_sum"].sem, g["kk_sum"].one())
    pe.wait_ge(g["gates_ready"].sem, g["gates_ready"].at(None, 2))
    wag = g["m_wag"]
    for n in range(2):
        for d in range(DIRS):
            lo, hi = d * 64, d * 64 + 64
            for c in range(NC):
                q = n * DN + d * NC + c
                if q == 0:
                    pe.wait_ge(g["p_out"].sem, g["p_out"].at(None, 20))
                elif q >= 4:
                    pe.wait_ge(g["lora_out"].sem, g["lora_out"].at(None, q - 3))
                w = g["w2d"] if n == 0 else g["a2i"]
                nc.tensor.matmul(flat[q % 4], w[lo:hi, c * P:(c + 1) * P], wag[lo:hi, n, :], start=True, stop=True).then_inc(
                    
                    g["lora_done"].sem, g["lora_done"].one())

    def halves(out, lhsT, rhs, start=True, stop=True):
        for lo in (0, 64):
            mm = nc.tensor.matmul(out[lo:lo + 64], lhsT[lo:lo + 64], rhs[lo:lo + 64], start=start, stop=stop)
        return mm

    def carry(bank):
        nc.tensor.matmul(bank[0:32, 0:2], g["c"]("ident")[:, 0:32], g["c"]("ident")[:, 0:2], start=True, stop=True)

    def step(turn, lat, i):
        wide = 2 * C2 if lat else C2
        pe.wait_ge(g["staged"].sem, g["staged"].at(turn, 2 if lat else 1))
        carry(flat[0])
        for q, (src, n) in enumerate((("sB", 0), ("sB", 1), ("sK", 0), ("sK", 1))):
            for j in range(NC):
                dc = n * NC + j
                mm = halves(flat[q][:, j * 2 * C2:j * 2 * C2 + wide], g[src][:, dc, :], g["sA"][:, dc, 0:wide])
            mm.then_inc(g["pairs_done"].sem, g["pairs_done"].one())
        pe.wait_ge(g["state_ready"].sem, g["state_ready"].at(turn, 0))
        if lat:
            pe.wait_ge(g["y_kept"].sem, g["y_kept"].at(i, 0))
        carry(flat[4])
        for dc in range(DN):
            mm = halves(flat[4][:, dc * C2:(dc + 1) * C2], g["sA"][:, dc, 0:C2], g["sB"][:, dc, :])
        mm.then_inc(g["first_done"].sem, g["first_done"].one())
        for q, src in enumerate(("sV", "sB", "sK")):
            for dc in range(DN):
                for lo in (0, 64):
                    mm = nc.tensor.matmul(flat[5 + q][lo:lo + 64, dc * C2:(dc + 1) * C2], g[src][lo:lo + 64, dc, :],
                                          g["c"]("ident")[lo:lo + 64, lo:lo + 64], start=True, stop=True)
            mm.then_inc(g["tok_done"].sem, g["tok_done"].one())
        pe.wait_ge(g["pairs_out"].sem, g["pairs_out"].at(turn, 4))
        pe.wait_ge(g["tok_out"].sem, g["tok_out"].at(turn, 3))
        carry(flat[7])
        for dc in range(DN):
            halves(flat[7][:, dc * C2:(dc + 1) * C2], g["sA"][:, dc, 0:C2], g["ST"][:, dc, :], True, False)
            mm = halves(flat[7][:, dc * C2:(dc + 1) * C2], g["NQ"][:, dc, 0:C2], g["tV"][:, dc, :], False, True)
        mm.then_inc(g["g0_done"].sem, g["g0_done"].one())
        pe.wait_ge(g["x_ready"].sem, g["x_ready"].at(turn, 1))
        for k in range(LEVELS):
            pe.wait_ge(g["levels_cut"].sem, g["levels_cut"].at(turn, k + 1))
            for d in range(DIRS):
                if k:
                    pe.wait_ge(g["x_next"].sem, g["x_next"].at(turn, 2 * (k - 1) + d + 1))
                carry(flat[d])
                for c in range(NC):
                    mm = halves(flat[d][:, c * C2:(c + 1) * C2], g["cut"][:, k, d * NC + c, :], g["XX"][:, d, 1, c, :])
                mm.then_inc(g["t_done"].sem, g["t_done"].one())
            for d in range(DIRS):
                pe.wait_ge(g["t_out"].sem, g["t_out"].at(turn, 2 * k + d + 1))
                carry(flat[2 + d])
                for c in range(NC):
                    mm = halves(flat[2 + d][:, c * C2:(c + 1) * C2], g["T1"][:, d * NC + c, :], g["XX"][:, d, 0, c, :])
                if k < LEVELS - 1:
                    for c in range(NC, 2 * NC):
                        mm = halves(flat[2 + d][:, c * C2:(c + 1) * C2], g["XX"][:, d, 0, c - NC, :],
                                    g["T1"][:, d * NC + c - NC, :])
                mm.then_inc(g["d_done"].sem, g["d_done"].one())
        pe.wait_ge(g["g0_out"].sem, g["g0_out"].at(turn, 1))
        for d in range(DIRS):
            pe.wait_ge(g["x_next"].sem, g["x_next"].at(turn, 2 * (LEVELS - 1) + d + 1))
            carry(flat[d])
            for c in range(NC):
                mm = halves(flat[d][:, c * C2:(c + 1) * C2], g["XX"][:, d, 0, c, :], g["G0"][:, d * NC + c, :])
            mm.then_inc(g["u_done"].sem, g["u_done"].one())
        for d in range(DIRS):
            pe.wait_ge(g["u_out"].sem, g["u_out"].at(turn, d + 1))
            out = flat[(7, 4)[d]]
            carry(out)
            for c in range(NC):
                dc = d * NC + c
                halves(out[:, c * C2:(c + 1) * C2], g["tB"][:, dc, :], g["U"][:, dc, :], True, False)
                mm = halves(out[:, c * C2:(c + 1) * C2], g["tK"][:, dc, :], g["tV"][:, dc, :], False, True)
            mm.then_inc(g["s_done"].sem, g["s_done"].one())
        if lat:
            for d in range(DIRS):
                for c in range(NC):
                    dc = d * NC + c
                    out = flat[5 + d][:, c * C2:(c + 1) * C2]
                    halves(out, g["ST"][:, dc, :], g["sA"][:, dc, C2:2 * C2], True, False)
                    halves(out, g["U"][:, dc, :], g["MP"][:, dc, C2:2 * C2], False, False)
                    mm = halves(out, g["tV"][:, dc, :], g["NQ"][:, dc, C2:2 * C2], False, True)
                mm.then_inc(g["y_step"].sem, g["y_step"].one())

    with pe.Fori(0, STEPS) as i:
        step(i, False, i)
    for name in ("tok_done", "pairs_done", "first_done", "t_done", "d_done", "g0_done", "u_done", "s_done"):
        g[name].n = 0
    with pe.Fori(0, STEPS) as i:
        step(i + STEPS, True, i)

    for d in range(DIRS):
        for c in range(NC):
            q = d * NC + c
            if q == 0:
                pe.wait_ge(g["state_ready"].sem, g["state_ready"].at(2 * STEPS - 1, 1))
            if q >= 2:
                pe.wait_ge(g["g_out"].sem, g["g_out"].at(None, q - 1))
            nc.tensor.matmul(flat[q % 2][:, 0:T], g["g2g"][:, d, c * P:(c + 1) * P], wag[:, 2 + d, 0:T],
                             start=True, stop=True).then_inc(g["g_done"].sem, g["g_done"].one())
    pe.wait_ge(g["y_kept"].sem, g["y_kept"].at(STEPS - 1, 1))
    yf = g["yy"][:, :, :].rearrange("p (n s) t -> p n (s t)", s=2)
    sq = g["squares"][:, 0:4, :]
    for n in range(4):
        nc.tensor.matmul(flat[2 + n], blk64, yf[:, n, :], start=True, stop=True).then_inc(
            g["gn_sum"].sem, g["gn_sum"].one())
    pe.wait_ge(g["bonus_ready"].sem, g["bonus_ready"].at(None, 1))
    for n in range(4):
        if n >= 2:
            pe.wait_ge(g["bonus_out"].sem, g["bonus_out"].at(None, n - 1))
        nc.tensor.matmul(flat[6 + n % 2], blk64, g["squares"][:, 4 + n, :], start=True, stop=True).then_inc(
            g["bonus_sum"].sem, g["bonus_sum"].one())
    pe.wait_ge(g["gn_centred"].sem, g["gn_centred"].at(None, 1))
    for n in range(4):
        nc.tensor.matmul(flat[2 + n], blk64, sq[:, n, :], start=True, stop=True).then_inc(
            g["gn_sum"].sem, g["gn_sum"].one())
    pe.wait_ge(g["g_out"].sem, g["g_out"].at(None, 8))
    for n in range(4):
        if n >= 2:
            pe.wait_ge(g["f_a_out"].sem, g["f_a_out"].at(None, n - 1))
        for t in range(TC):
            mm = nc.tensor.matmul(flat[n % 2][:, t * T:(t + 1) * T], g["m_f"][:, n, t * P:(t + 1) * P], g["mc"]("chan"),
                                  start=True, stop=True)
        mm.then_inc(g["f_a"].sem, g["f_a"].one())
    fa = g["fa"]
    pe.wait_ge(g["bonus_out"].sem, g["bonus_out"].at(None, 4))
    pe.wait_ge(g["f_a_out"].sem, g["f_a_out"].at(None, 4))
    for n in range(2):
        for j in range(2):
            c = 2 * n + j
            for t in range(TC):
                for part in range(2):
                    w = g["mc"](("timeC", "timeS")[part])[:, t * T:(t + 1) * T]
                    mm = nc.tensor.matmul(flat[6 + n][:, j * T:(j + 1) * T], fa[:, c, t, part * P:(part + 1) * P], w,
                                          start=(t == 0 and part == 0), stop=(t == 1 and part == 1))
        mm.then_inc(g["f_b"].sem, g["f_b"].one())
    pe.wait_ge(g["f_b_out"].sem, g["f_b_out"].at(None, 2))
    for n in range(2):
        for j in range(2):
            c = 2 * n + j
            mm = nc.tensor.matmul(flat[n][:, j * T:(j + 1) * T], g["wf"][:, c, :], g["spec"][:, c, :],
                                  start=True, stop=True)
        mm.then_inc(g["f_c"].sem, g["f_c"].one())
    pe.wait_ge(g["f_c_out"].sem, g["f_c_out"].at(None, 2))
    pe.wait_ge(g["gn_root"].sem, g["gn_root"].at(None, 4))

    def project(i, chunks):
        w = slot(ADA_UNITS + IN_UNITS + i // 2)
        for j in range(2):
            col = (i % 2) * 2 * P + j * P
            for k in chunks:
                mm = nc.tensor.matmul(g["bank"][2 + i][:, j, :], w[:, k, col:col + P], g["cat"][:, k, :],
                                      start=(j == 0 and k == NC), stop=(k == NC - 1), skip_group_check=True)
        return mm

    for i in range(4):
        project(i, range(NC, DC))
    pe.wait_ge(g["cat_ready"].sem, g["cat_ready"].at(None, 1))
    for i in range(4):
        project(i, range(NC)).then_inc(g["mo_done"].sem, g["mo_done"].one())
    pe.wait_ge(g["mo_out"].sem, g["mo_out"].at(None, 4))
    for c in range(DC):
        mm = nc.tensor.matmul(g["bank"][0][:, 0, :], ones, g["xT"][:, c, :], start=(c == 0), stop=(c == DC - 1))
    mm.then_inc(g["ln_sum"].sem, g["ln_sum"].one())
    pe.wait_ge(g["res_squared"].sem, g["res_squared"].at(None, 1))
    for c in range(DC):
        mm = nc.tensor.matmul(g["bank"][1][:, 0, :], ones, g["squares"][:, c, 0:T], start=(c == 0), stop=(c == DC - 1))
    mm.then_inc(g["ln_sum"].sem, g["ln_sum"].one())


def latent_only(q):
    return q < 4 or q >= 14


def mixer_scalar(act, nc, g):
    flat = [b[:, :, :].rearrange("p a b -> p (a b)") for b in g["bank"]]
    mp = g["mpar"]

    def par(name, i=0):
        return mp[:, MIX_PAR[name] + i:MIX_PAR[name] + i + 1]

    act.wait_ge(g["y_out"].sem, g["y_out"].at(None, DEPTH * Y_PAIRS))
    for u in range(ADA_UNITS):
        act.wait_ge(g["ada_unit"].sem, g["ada_unit"].at(None, u + 1))
        nc.scalar.activation(g["rows"][0:2, u * UNIT:(u + 1) * UNIT], flat[5 + u % 2][0:2, :], ACT.Copy).then_inc(
            g["row_out"].sem, g["row_out"].one())
        if u == 6:
            act.wait_ge(g["ln_sum"].sem, g["ln_sum"].at(None, 2))
            nc.scalar.activation(g["lnrow"][:, 0, :], flat[2], ACT.Sqrt, bias=g["eps2"][:, 0:1], scale=1.0 / D).then_inc(
                g["ln_root"].sem, g["ln_root"].one())

    def lat_inside(j):
        return g["lat_pad"][:, j, 1:GRID_H + 1, 1:GRID_W + 1]

    for q in range(20):
        act.wait_ge(g["p_done"].sem, g["p_done"].at(None, q + 1))
        u, j = q // 4, q % 4
        if j == 0 and 0 < u < 4:
            act.wait_ge(g["shifted"].sem, g["shifted"].at(None, u))
        if u == 4:
            ins = nc.scalar.activation(g["m_f"][:, j, :], flat[q % 4][:, 0:T], ACT.Copy)
        else:
            lo = 0 if latent_only(q) else T
            if not latent_only(q):
                nc.scalar.activation(g["ctx_pad"][:, j, 1:T + 1], flat[q % 4][:, 0:T], ACT.Copy)
            ins = nc.scalar.activation(lat_inside(j), flat[q % 4][:, lo:lo + T].rearrange("p (a b) -> p a b", a=GRID_H), ACT.Copy)
        ins.then_inc(g["p_out"].sem, g["p_out"].one())
    for c in range(NC):
        act.wait_ge(g["kk_sum"].sem, g["kk_sum"].at(None, c + 1))
        nc.scalar.activation(g["squares"][:, 4 + c, :], flat[4 + c], ACT.Sqrt).then_inc(
            g["kk_root"].sem, g["kk_root"].one())
    act.wait_ge(g["shifted"].sem, g["shifted"].at(None, 4))
    wag = g["m_wag"]
    nc.scalar.activation(wag[:, 0, :], wag[:, 0, :], ACT.Tanh).then_inc(g["gates_ready"].sem, g["gates_ready"].one())
    nc.scalar.activation(wag[:, 2:4, 0:T], wag[:, 2:4, 0:T], ACT.Sigmoid).then_inc(
        g["gates_ready"].sem, g["gates_ready"].one())
    for q in range(16):
        act.wait_ge(g["lora_done"].sem, g["lora_done"].at(None, q + 1))
        dst, name = (g["stack"], "w0") if q < DN else (g["iclr"], "a0")
        nc.scalar.activation(dst[:, q % DN, :], flat[q % 4], ACT.Sigmoid, bias=par(name, q % DN)).then_inc(
            g["lora_out"].sem, g["lora_out"].one())
    act.wait_ge(g["decay_set"].sem, g["decay_set"].at(None, 1))
    for d in range(DIRS):
        incl = g["incl"][d]
        nc.scalar.activation(g["grow"][:, d * NC:(d + 1) * NC, :], incl[:, :, T:2 * T], ACT.Exp)
        ins = nc.scalar.activation(g["excl"][d], g["excl"][d], ACT.Exp)
    ins = nc.scalar.activation(g["total"][:, :, :], g["total"][:, :, :], ACT.Exp)
    ins.then_inc(g["exps_ready"].sem, g["exps_ready"].one())
    act.wait_ge(g["exps_ready"].sem, g["exps_ready"].at(None, 1))
    for d in range(DIRS):
        ins = nc.scalar.activation(g["incl"][d], g["incl"][d], ACT.Exp, scale=-1.0)
    ins.then_inc(g["exps_ready"].sem, g["exps_ready"].one())

    def step(turn, lat, i):
        for q, name in enumerate(("tV", "tB", "tK")):
            act.wait_ge(g["tok_done"].sem, g["tok_done"].at(turn, q + 1))
            nc.scalar.activation(g[name].rearrange("p n w -> p (n w)"), flat[5 + q], ACT.Copy).then_inc(
                g["tok_out"].sem, g["tok_out"].one())
        act.wait_ge(g["g0_done"].sem, g["g0_done"].at(turn, 1))
        nc.scalar.activation(g["G0"].rearrange("p n w -> p (n w)"), flat[7], ACT.Copy).then_inc(
            g["g0_out"].sem, g["g0_out"].one())

        def direction(name, d):
            return g[name][:, d * NC:(d + 1) * NC, :].rearrange("p n w -> p (n w)")

        for k in range(LEVELS):
            for d in range(DIRS):
                act.wait_ge(g["t_done"].sem, g["t_done"].at(turn, 2 * k + d + 1))
                nc.scalar.activation(direction("T1", d), flat[d][:, 0:NC * C2], ACT.Copy).then_inc(
                    g["t_out"].sem, g["t_out"].one())
        for d in range(DIRS):
            act.wait_ge(g["u_done"].sem, g["u_done"].at(turn, d + 1))
            nc.scalar.activation(direction("U", d), flat[d][:, 0:NC * C2], ACT.Copy).then_inc(
                g["u_out"].sem, g["u_out"].one())
        if lat:
            for d in range(DIRS):
                act.wait_ge(g["y_step"].sem, g["y_step"].at(i, d + 1))
                t0 = i * C2 if d == 0 else (STEPS - 1) * C2 - i * C2
                ins = nc.scalar.activation(g["yy"][:, d * NC:(d + 1) * NC, bass.ds(t0, C2)],
                                           flat[5 + d][:, 0:NC * C2].rearrange("p (n w) -> p n w", n=NC), ACT.Copy)
            ins.then_inc(g["y_kept"].sem, g["y_kept"].one())

    act.sem_inc(g["y_kept"].sem, g["y_kept"].base)
    with act.Fori(0, STEPS) as i:
        step(i, False, i)
    for name in ("tok_out", "g0_out", "t_out", "u_out"):
        g[name].n = 0
    with act.Fori(0, STEPS) as i:
        step(i + STEPS, True, i)

    for q in range(8):
        act.wait_ge(g["g_done"].sem, g["g_done"].at(None, q + 1))
        nc.scalar.activation(g["gate"][:, q, :], flat[q % 2][:, 0:T], ACT.Copy).then_inc(
            g["g_out"].sem, g["g_out"].one())
    for n in range(4):
        act.wait_ge(g["bonus_sum"].sem, g["bonus_sum"].at(None, n + 1))
        nc.scalar.activation(g["bonus"][:, n, :], flat[6 + n % 2], ACT.Copy).then_inc(
            g["bonus_out"].sem, g["bonus_out"].one())
    for n in range(4):
        act.wait_ge(g["f_a"].sem, g["f_a"].at(None, n + 1))
        nc.scalar.activation(g["fa"][:, n].rearrange("p a b -> p (a b)"), flat[n % 2], ACT.Copy).then_inc(
            g["f_a_out"].sem, g["f_a_out"].one())
    for n in range(4):
        act.wait_ge(g["gn_sum"].sem, g["gn_sum"].at(None, 5 + n))
        nc.scalar.activation(g["squares"][:, n, :], flat[2 + n], ACT.Sqrt, bias=g["eps2"][:, 1:2], scale=1.0 / C2).then_inc(
            
            g["gn_root"].sem, g["gn_root"].one())
    for n in range(2):
        act.wait_ge(g["f_b"].sem, g["f_b"].at(None, n + 1))
        nc.scalar.activation(g["spec"][:, 2 * n:2 * n + 2, :], g["bank"][6 + n][:, :, :], ACT.Copy).then_inc(
            g["f_b_out"].sem, g["f_b_out"].one())
    for n in range(2):
        act.wait_ge(g["f_c"].sem, g["f_c"].at(None, n + 1))
        for j in range(2):
            c = 2 * n + j
            ins = nc.scalar.activation(g["cat"][:, NC + c, :], g["bank"][n][:, j, :], ACT.Identity, bias=par("b_fno", c))
        ins.then_inc(g["f_c_out"].sem, g["f_c_out"].one())
    act.wait_ge(g["ln_sum"].sem, g["ln_sum"].at(None, 4))
    nc.scalar.activation(g["lnrow"][:, 0, 0:T], g["bank"][1][:, 0, :], ACT.Sqrt, bias=g["eps2"][:, 0:1], scale=1.0 / D).then_inc(
        
        g["ln_root"].sem, g["ln_root"].one())


def mixer_aliases(g):
    g["rows"] = g["early"][:, 0:2 * DN, :].rearrange("p n t -> p (n t)")[:, 0:ADA_UNITS * UNIT]
    g["lnrow"] = g["early"][:, 3 * DN // 2:3 * DN // 2 + 2, :]
    g["cat"] = g["stack"][:, :, 0:T]
    g["incl"] = [g["squares"][:, 0:NC, :], g["stack"][:, NC:DN, :]]
    g["excl"] = [g["stack"][:, 0:NC, :], g["squares"][:, NC:DN, :]]
    g["gate"] = g["stack"][:, :, T:2 * T]
    g["bonus"] = g["iclr"][:, 0:4, :]
    g["fa"] = g["iclr"][:, 4:8, :].rearrange("p c (t w) -> p c t w", t=TC)
    g["spec"] = g["kk"][:, :, 0:T]


def mixer_vector(dve, nc, g):
    v = nc.vector
    flat = [b[:, :, :].rearrange("p a b -> p (a b)") for b in g["bank"]]
    mp, stack, squares, xT = g["mpar"], g["stack"], g["squares"], g["xT"]
    init = g["init_dve"]

    def par(name, i=0):
        return mp[:, MIX_PAR[name] + i:MIX_PAR[name] + i + 1]

    mod = g["mod"]
    v.memset(g["eps2"][:, 0:1], LN_EPS)
    v.memset(g["eps2"][:, 1:2], GN_EPS)
    v.memset(g["lat_pad"][:, :, :, :], 0.0)
    v.memset(g["ctx_pad"][:, :, :], 0.0)
    dve.wait_ge(g["mix_in"].sem, g["mix_in"].at(None, 7))
    v.tensor_copy(stack[:, :, T:2 * T], xT[:, :, :]).then_inc(g["stack_ready"].sem, g["stack_ready"].one())
    dve.wait_ge(g["ln_sum"].sem, g["ln_sum"].at(None, 1))
    v.tensor_scalar(g["lnrow"][:, 1, :], flat[1], 1.0 / D, None, ALU.mult).then_inc(
        g["init_dve"].sem, g["init_dve"].one())
    dve.wait_ge(g["init_dve"].sem, g["init_dve"].now(None))
    v.tensor_tensor(stack[:, :, :], stack[:, :, :], row(g["lnrow"][:, 1, :], DC), ALU.subtract).then_inc(
        g["init_dve"].sem, g["init_dve"].one())
    dve.wait_ge(g["init_dve"].sem, g["init_dve"].now(None))
    v.tensor_tensor(squares[:, :, :], stack[:, :, :], stack[:, :, :], ALU.mult).then_inc(
        g["ln_centred"].sem, g["ln_centred"].one())
    dve.wait_ge(g["ln_root"].sem, g["ln_root"].at(None, 1))
    v.reciprocal(g["lnrow"][:, 0, :], g["lnrow"][:, 0, :]).then_inc(g["init_dve"].sem, g["init_dve"].one())
    dve.wait_ge(g["init_dve"].sem, g["init_dve"].now(None))
    v.tensor_tensor(stack[:, :, :], stack[:, :, :], row(g["lnrow"][:, 0, :], DC), ALU.mult).then_inc(
        g["init_dve"].sem, g["init_dve"].one())
    dve.wait_ge(g["init_dve"].sem, g["init_dve"].now(None))
    for c in range(DC):
        ins = v.tensor_scalar(stack[:, c, :], stack[:, c, :], par("ln0_g", c), par("ln0_b", c), ALU.mult, ALU.add)
    ins.then_inc(g["init_dve"].sem, g["init_dve"].one())
    dve.wait_ge(g["init_dve"].sem, g["init_dve"].now(None))
    v.tensor_copy(xT[:, :, :], stack[:, :, T:2 * T])
    dve.wait_ge(g["mod_turned"].sem, g["mod_turned"].at(None, 1))
    b_ada = mp[:, MIX_PAR["b_ada"]:MIX_PAR["b_ada"] + 6 * DC].unsqueeze(2).to_broadcast([P, 6 * DC, 2])
    v.tensor_tensor(mod[:, :, :], flat[4][:, 0:12 * DC].rearrange("p (n s) -> p n s", s=2), b_ada, ALU.add).then_inc(
        g["init_dve"].sem, g["init_dve"].one())
    dve.wait_ge(g["init_dve"].sem, g["init_dve"].now(None))
    for a in (SC1, SC2):
        ins = v.tensor_scalar(mod[:, a:a + DC, :], mod[:, a:a + DC, :], 1.0, None, ALU.add)
    ins.then_inc(g["init_dve"].sem, g["init_dve"].one())
    dve.wait_ge(g["init_dve"].sem, g["init_dve"].now(None))
    for c in range(DC):
        for s in range(2):
            part = stack[:, c, (1 - s) * T:(2 - s) * T]
            ins = v.tensor_scalar(part, part, mod[:, SC1 + c, s:s + 1], mod[:, SH1 + c, s:s + 1], ALU.mult, ALU.add)
    ins.then_inc(g["h2_ready"].sem, g["h2_ready"].one())
    lat, ctxp, near = g["lat_pad"], g["ctx_pad"], g["near"]
    mk, kk, iclr, kd = g["m_k"], g["kk"], g["iclr"], g["kd"]
    for u in range(4):
        dve.wait_ge(g["p_out"].sem, g["p_out"].at(None, 4 * u + 4))
        dst = (g["m_r"], g["m_k"], g["m_v"], g["m_wag"])[u]
        for j in range(NC):
            grid = lat[:, j]
            n0 = near[:, 0, j, :].rearrange("p (a b) -> p a b", a=GRID_H)
            n1 = near[:, 1, j, :].rearrange("p (a b) -> p a b", a=GRID_H)
            v.tensor_tensor(n0, grid[:, 0:GRID_H, 1:GRID_W + 1], grid[:, 2:GRID_H + 2, 1:GRID_W + 1], ALU.add)
            ins = v.tensor_tensor(n1, grid[:, 1:GRID_H + 1, 0:GRID_W], grid[:, 1:GRID_H + 1, 2:GRID_W + 2], ALU.add)
        ins.then_inc(g["init_dve"].sem, g["init_dve"].one())
        dve.wait_ge(g["init_dve"].sem, g["init_dve"].now(None))
        v.tensor_tensor(near[:, 0], near[:, 0], near[:, 1], ALU.add).then_inc(g["init_dve"].sem, g["init_dve"].one())
        dve.wait_ge(g["init_dve"].sem, g["init_dve"].now(None))
        for j in range(NC):
            inside = lat[:, j, 1:GRID_H + 1, 1:GRID_W + 1]
            n0 = near[:, 0, j, :].rearrange("p (a b) -> p a b", a=GRID_H)
            ins = v.scalar_tensor_tensor(out=n0, in0=n0, scalar=0.25, in1=inside, op0=ALU.mult, op1=ALU.subtract)
        ins.then_inc(g["init_dve"].sem, g["init_dve"].one())
        dve.wait_ge(g["init_dve"].sem, g["init_dve"].now(None))
        for j in range(NC):
            q = 4 * u + j
            lo = 0 if latent_only(q) else T
            inside = lat[:, j, 1:GRID_H + 1, 1:GRID_W + 1]
            n0 = near[:, 0, j, :].rearrange("p (a b) -> p a b", a=GRID_H)
            ins = v.scalar_tensor_tensor(out=dst[:, j, lo:lo + T].rearrange("p (a b) -> p a b", a=GRID_H), in0=n0,
                                         scalar=par("mu", q), in1=inside, op0=ALU.mult, op1=ALU.add)
        js = [j for j in range(NC) if not latent_only(4 * u + j)]
        if js:
            n = len(js)
            v.tensor_tensor(near[:, 1, 0:n], ctxp[:, 0:n, 0:T], ctxp[:, 0:n, 2:T + 2], ALU.add).then_inc(
                g["init_dve"].sem, g["init_dve"].one())
            dve.wait_ge(g["init_dve"].sem, g["init_dve"].now(None))
            v.scalar_tensor_tensor(out=near[:, 1, 0:n], in0=near[:, 1, 0:n], scalar=0.5, in1=ctxp[:, 0:n, 1:T + 1],
                                   op0=ALU.mult, op1=ALU.subtract).then_inc(g["init_dve"].sem, g["init_dve"].one())
            dve.wait_ge(g["init_dve"].sem, g["init_dve"].now(None))
            for j in js:
                ins = v.scalar_tensor_tensor(out=dst[:, j, 0:T], in0=near[:, 1, j, :], scalar=par("mu", 4 * u + j),
                                             in1=ctxp[:, j, 1:T + 1], op0=ALU.mult, op1=ALU.add)
        ins.then_inc(g["shifted"].sem, g["shifted"].one())
        if u == 1:
            dve.wait_ge(g["shifted"].sem, g["shifted"].at(None, 2))
            for c in range(NC):
                ins = v.tensor_scalar(kk[:, c, :], mk[:, c, :], par("k_k", c), None, ALU.mult)
            ins.then_inc(g["init_dve"].sem, g["init_dve"].one())
            dve.wait_ge(g["init_dve"].sem, g["init_dve"].now(None))
            v.tensor_tensor(squares[:, 0:NC, :], kk[:, :, :], kk[:, :, :], ALU.mult).then_inc(
                g["kk_squared"].sem, g["kk_squared"].one())
    dve.wait_ge(g["shifted"].sem, g["shifted"].at(None, 4))
    dve.wait_ge(g["kk_root"].sem, g["kk_root"].at(None, 4))
    v.tensor_scalar(squares[:, 4:8, :], squares[:, 4:8, :], 1e-12, None, ALU.max).then_inc(
        g["init_dve"].sem, g["init_dve"].one())
    dve.wait_ge(g["init_dve"].sem, g["init_dve"].now(None))
    v.reciprocal(squares[:, 4:8, :], squares[:, 4:8, :]).then_inc(g["init_dve"].sem, g["init_dve"].one())
    dve.wait_ge(g["init_dve"].sem, g["init_dve"].now(None))
    v.tensor_tensor(kk[:, :, :], kk[:, :, :], squares[:, 4:8, :], ALU.mult).then_inc(
        g["init_dve"].sem, g["init_dve"].one())
    dve.wait_ge(g["init_dve"].sem, g["init_dve"].now(None))
    dve.wait_ge(g["lora_out"].sem, g["lora_out"].at(None, DN))
    v.tensor_scalar(stack[:, :, :], stack[:, :, :], LOG_W, None, ALU.mult).then_inc(
        g["init_dve"].sem, g["init_dve"].one())
    dve.wait_ge(g["init_dve"].sem, g["init_dve"].now(None))
    for dc in range(DN):
        ins = v.tensor_tensor_scan(squares[:, dc, :], g["mc"]("reset"), stack[:, dc, :], 0.0, ALU.mult, ALU.add)
    ins.then_inc(g["init_dve"].sem, g["init_dve"].one())
    dve.wait_ge(g["init_dve"].sem, g["init_dve"].now(None))
    ends = squares[:, :, :].rearrange("p n (m t) -> p n m t", t=C2)[:, :, :, C2 - 1]
    v.tensor_copy(g["total"][:, :, :], ends).then_inc(g["init_dve"].sem, g["init_dve"].one())
    dve.wait_ge(g["init_dve"].sem, g["init_dve"].now(None))
    for dc in range(NC, DN):
        part = squares[:, dc, :].rearrange("p (m t) -> p m t", t=C2)
        tot = g["total"][:, dc, :].unsqueeze(2).to_broadcast([P, 2 * STEPS, C2])
        ins = v.tensor_tensor(part, tot, part, ALU.subtract)
    ins.then_inc(g["init_dve"].sem, g["init_dve"].one())
    dve.wait_ge(g["init_dve"].sem, g["init_dve"].now(None))
    v.tensor_tensor(stack[:, 0:NC, :], squares[:, 0:NC, :], stack[:, 0:NC, :], ALU.subtract)
    v.tensor_tensor(stack[:, NC:DN, :], squares[:, NC:DN, :], stack[:, NC:DN, :], ALU.add).then_inc(
        g["decay_set"].sem, g["decay_set"].one())
    dve.wait_ge(g["lora_out"].sem, g["lora_out"].at(None, 2 * DN))
    for dc in range(DN):
        ins = v.tensor_scalar(kd[:, dc, :], iclr[:, dc, :], 1.0, par("k_a", dc % NC), ALU.subtract, ALU.mult)
    ins.then_inc(g["init_dve"].sem, g["init_dve"].one())
    dve.wait_ge(g["init_dve"].sem, g["init_dve"].now(None))
    for d in range(DIRS):
        half = kd[:, d * NC:(d + 1) * NC, :]
        ins = v.scalar_tensor_tensor(out=half, in0=half, scalar=1.0, in1=mk[:, :, :], op0=ALU.add, op1=ALU.mult)
        b = iclr[:, d * NC:(d + 1) * NC, :]
        ins = v.tensor_tensor(b, b, kk[:, :, :], ALU.mult)
    ins.then_inc(g["init_dve"].sem, g["init_dve"].one())
    dve.wait_ge(g["init_dve"].sem, g["init_dve"].now(None))
    v.memset(g["ST"][:, :, :], 0.0).then_inc(g["state_ready"].sem, g["state_ready"].base)
    dve.wait_ge(g["exps_ready"].sem, g["exps_ready"].at(None, 2))

    def stage(lat_, i):
        for d in range(DIRS):
            h = slice(d * NC, (d + 1) * NC)
            s = bass.ds(chunk_start(lat_, i, d), C2)
            v.scalar_tensor_tensor(out=g["sA"][:, h, 0:C2], in0=kk[:, :, s], scalar=-1.0, in1=g["excl"][d][:, :, s],
                                   op0=ALU.mult, op1=ALU.mult)
            v.tensor_tensor(g["sB"][:, h, :], iclr[:, h, s], g["incl"][d][:, :, s], ALU.mult)
            v.tensor_tensor(g["sK"][:, h, :], kd[:, h, s], g["incl"][d][:, :, s], ALU.mult)
            ins = v.tensor_copy(g["sV"][:, h, :], g["m_v"][:, :, s])
        return ins

    def stage_r(i):
        for d in range(DIRS):
            h = slice(d * NC, (d + 1) * NC)
            s = bass.ds(chunk_start(False, i, d), C2)
            ins = v.tensor_tensor(g["sA"][:, h, C2:2 * C2], g["m_r"][:, :, s], g["grow"][:, h, s], ALU.mult)
        return ins

    def step(turn, lat_, i, chained):
        steps = g[chained]
        wide = 2 * C2 if lat_ else C2
        keep = g["mc"]("keep").rearrange("p (d w) -> p d w", d=DIRS)
        for q in range(4):
            dve.wait_ge(g["pairs_done"].sem, g["pairs_done"].at(turn, q + 1))
            d = q % 2
            dst = g["MP"] if q < 2 else g["NQ"]
            v.tensor_tensor(dst[:, d * NC:(d + 1) * NC, 0:wide],
                            flat[q].rearrange("p (n w) -> p n w", n=NC)[:, :, 0:wide], row(keep[:, d, 0:wide], NC),
                            ALU.mult).then_inc(g["pairs_out"].sem, g["pairs_out"].one())
        dve.wait_ge(g["first_done"].sem, g["first_done"].at(turn, 1))
        dve.wait_ge(g["pairs_out"].sem, g["pairs_out"].at(turn, 4))
        first = g["mc"]("first").rearrange("p (d w) -> p d w", d=DIRS)
        for d in range(DIRS):
            h = slice(d * NC, (d + 1) * NC)
            v.tensor_tensor(g["XX"][:, d, 1], flat[4].rearrange("p (n w) -> p n w", n=DN)[:, h, :], row(first[:, d, :], NC),
                            ALU.mult)
            ins = v.tensor_tensor(g["XX"][:, d, 0], g["MP"][:, h, 0:C2], row(first[:, 1 - d, :], NC), ALU.mult)
        ins.then_inc(steps.sem, steps.one())
        dve.wait_ge(steps.sem, steps.now(i))
        every = g["XX"].rearrange("p d s c w -> p (d s c) w")
        v.tensor_tensor(every, every, row(g["mc"]("eye"), 2 * DN), ALU.add).then_inc(
            g["x_ready"].sem, g["x_ready"].one())
        for k in range(LEVELS):
            for d in range(DIRS):
                dve.wait_ge(g["d_done"].sem, g["d_done"].at(turn, 2 * k + d + 1))
                if k:
                    dve.wait_ge(g["x_next"].sem, g["x_next"].at(turn, 2 * (k - 1) + d + 1))
                else:
                    dve.wait_ge(g["x_ready"].sem, g["x_ready"].at(turn, 1))
                n = 2 * NC if k < LEVELS - 1 else NC
                x = g["XX"][:, d].rearrange("p s c w -> p (s c w)")[:, 0:n * C2]
                v.tensor_tensor(x, x, flat[2 + d][:, 0:n * C2], ALU.add).then_inc(g["x_next"].sem, g["x_next"].one())
        ins = stage(lat_, (i + 1) % STEPS)
        if not lat_:
            ins.then_inc(g["staged"].sem, g["staged"].one())
        for d in range(DIRS):
            dve.wait_ge(g["s_done"].sem, g["s_done"].at(turn, d + 1))
            h = slice(d * NC, (d + 1) * NC)
            ins = v.tensor_tensor(g["sum"][:, h, :], g["ST"][:, h, :],
                                  flat[(7, 4)[d]][:, 0:NC * C2].rearrange("p (n w) -> p n w", n=NC), ALU.add)
        ins.then_inc(steps.sem, steps.one())
        dve.wait_ge(steps.sem, steps.now(i))
        if lat_:
            dve.wait_ge(g["y_step"].sem, g["y_step"].at(i, 2))
        for d in range(DIRS):
            h = slice(d * NC, (d + 1) * NC)
            m = (STEPS if lat_ else 0) + (i if d == 0 else STEPS - 1 - i)
            tot = g["total"][:, h, bass.ds(m, 1)].to_broadcast([P, NC, C2])
            ins = v.tensor_tensor(g["ST"][:, h, :], g["sum"][:, h, :], tot, ALU.mult)
        ins.then_inc(g["state_ready"].sem, g["state_ready"].one())
        if lat_:
            stage_r((i + 1) % STEPS).then_inc(g["staged"].sem, g["staged"].one())
        dve.wait_ge(g["state_ready"].sem, g["state_ready"].at(turn, 1))

    stage(False, 0).then_inc(g["staged"].sem, g["staged"].unit)
    with dve.Fori(0, STEPS) as i:
        step(i, False, i, "ctx_dve")
    for name in ("staged", "pairs_out", "x_ready", "x_next", "state_ready"):
        g[name].n = 0
    stage(True, 0)
    stage_r(0).then_inc(g["staged"].sem, g["staged"].unit)
    with dve.Fori(0, STEPS) as i:
        step(i + STEPS, True, i, "lat_dve")

    for dc in range(DN):
        d, c = dc // NC, dc % NC
        out = squares[:, 4 + dc // 2, (dc % 2) * T:(dc % 2 + 1) * T]
        ins = v.scalar_tensor_tensor(out=out, in0=g["m_r"][:, c, :], scalar=par("r_k", dc), in1=kd[:, dc, T:2 * T],
                                     op0=ALU.mult, op1=ALU.mult)
    ins.then_inc(g["bonus_ready"].sem, g["bonus_ready"].one())
    dve.wait_ge(g["gn_sum"].sem, g["gn_sum"].at(None, 4))
    yf = g["yy"][:, :, :].rearrange("p (n s) t -> p n (s t)", s=2)
    for n in range(4):
        ins = v.scalar_tensor_tensor(out=yf[:, n, :], in0=flat[2 + n], scalar=-1.0 / C2, in1=yf[:, n, :], op0=ALU.mult,
                                     op1=ALU.add)
    ins.then_inc(g["init_dve"].sem, g["init_dve"].one())
    dve.wait_ge(g["init_dve"].sem, g["init_dve"].now(None))
    v.tensor_tensor(squares[:, 0:4, :], yf, yf, ALU.mult).then_inc(g["gn_centred"].sem, g["gn_centred"].one())
    dve.wait_ge(g["gn_root"].sem, g["gn_root"].at(None, 4))
    v.reciprocal(squares[:, 0:4, :], squares[:, 0:4, :]).then_inc(g["init_dve"].sem, g["init_dve"].one())
    dve.wait_ge(g["init_dve"].sem, g["init_dve"].now(None))
    v.tensor_tensor(yf, yf, squares[:, 0:4, :], ALU.mult).then_inc(g["init_dve"].sem, g["init_dve"].one())
    dve.wait_ge(g["init_dve"].sem, g["init_dve"].now(None))
    for dc in range(DN):
        ins = v.tensor_scalar(g["yy"][:, dc, :], g["yy"][:, dc, :], par("gn_g", dc % NC), par("gn_b", dc % NC), ALU.mult, ALU.add)
    dve.wait_ge(g["bonus_out"].sem, g["bonus_out"].at(None, 4))
    bonus = g["bonus"].rearrange("p n (s t) -> p (n s) t", s=2)
    for d in range(DIRS):
        h = slice(d * NC, (d + 1) * NC)
        ins = v.tensor_tensor(bonus[:, h, :], bonus[:, h, :], g["m_v"][:, :, T:2 * T], ALU.mult)
    ins.then_inc(g["init_dve"].sem, g["init_dve"].one())
    dve.wait_ge(g["init_dve"].sem, g["init_dve"].now(None))
    v.tensor_tensor(g["yy"][:, :, :], g["yy"][:, :, :], bonus, ALU.add).then_inc(g["init_dve"].sem, g["init_dve"].one())
    dve.wait_ge(g["init_dve"].sem, g["init_dve"].now(None))
    dve.wait_ge(g["g_out"].sem, g["g_out"].at(None, 8))
    v.tensor_tensor(g["yy"][:, :, :], g["yy"][:, :, :], g["gate"], ALU.mult).then_inc(
        g["init_dve"].sem, g["init_dve"].one())
    dve.wait_ge(g["init_dve"].sem, g["init_dve"].now(None))
    v.tensor_tensor(g["cat"][:, 0:NC, :], g["yy"][:, 0:NC, :], g["yy"][:, NC:DN, :], ALU.add).then_inc(
        g["cat_ready"].sem, g["cat_ready"].one())
    for i in range(4):
        dve.wait_ge(g["mo_done"].sem, g["mo_done"].at(None, i + 1))
        for j in range(2):
            c = 2 * i + j
            ins = v.tensor_scalar(squares[:, c, 0:T], g["bank"][2 + i][:, j, :], mod[:, GT1 + c, 0:1], None, ALU.mult)
        ins.then_inc(g["init_dve"].sem, g["init_dve"].one())
        dve.wait_ge(g["init_dve"].sem, g["init_dve"].now(None))
        both = xT[:, 2 * i:2 * i + 2, :]
        v.scalar_tensor_tensor(out=both, in0=both, scalar=ALPHA, in1=squares[:, 2 * i:2 * i + 2, 0:T], op0=ALU.mult,
                               op1=ALU.add).then_inc(g["mo_out"].sem, g["mo_out"].one())
    dve.wait_ge(g["ln_sum"].sem, g["ln_sum"].at(None, 3))
    v.tensor_scalar(g["lnrow"][:, 1, 0:T], g["bank"][0][:, 0, :], 1.0 / D, None, ALU.mult).then_inc(
        g["init_dve"].sem, g["init_dve"].one())
    dve.wait_ge(g["init_dve"].sem, g["init_dve"].now(None))
    v.tensor_tensor(xT[:, :, :], xT[:, :, :], row(g["lnrow"][:, 1, 0:T], DC), ALU.subtract).then_inc(
        g["init_dve"].sem, g["init_dve"].one())
    dve.wait_ge(g["init_dve"].sem, g["init_dve"].now(None))
    v.tensor_tensor(squares[:, :, 0:T], xT[:, :, :], xT[:, :, :], ALU.mult).then_inc(
        g["res_squared"].sem, g["res_squared"].one())
    dve.wait_ge(g["ln_root"].sem, g["ln_root"].at(None, 2))
    v.reciprocal(g["lnrow"][:, 0, 0:T], g["lnrow"][:, 0, 0:T]).then_inc(g["init_dve"].sem, g["init_dve"].one())
    dve.wait_ge(g["init_dve"].sem, g["init_dve"].now(None))
    v.tensor_tensor(xT[:, :, :], xT[:, :, :], row(g["lnrow"][:, 0, 0:T], DC), ALU.mult).then_inc(
        g["init_dve"].sem, g["init_dve"].one())
    dve.wait_ge(g["init_dve"].sem, g["init_dve"].now(None))
    for c in range(DC):
        ins = v.tensor_scalar(xT[:, c, :], xT[:, c, :], par("ln1_g", c), par("ln1_b", c), ALU.mult, ALU.add)
    ins.then_inc(g["x_mixed"].sem, g["x_mixed"].one())
    dve.wait_ge(g["x_mixed"].sem, g["x_mixed"].at(None, 1))


N_EXPERTS = 32
TOP_K = 4
D_FF = 1024
FC = D_FF // P
SLOTS = 80
MAX_ROUNDS = -(-T // SLOTS)
E_UNITS = 6
BANK6, BANK7 = 5, 3
LIMIT, SIG_ALPHA = 7.0, 1.702

MOE_CONST = {}
MOE_CONST_WIDTH = 0
for _name, _width in (("tri", P), ("slot", SLOTS), ("b_router", N_EXPERTS), ("b1", N_EXPERTS * 2 * FC)):
    MOE_CONST[_name] = (MOE_CONST_WIDTH, MOE_CONST_WIDTH + _width)
    MOE_CONST_WIDTH += _width


def moe_constants():
    part = np.arange(P)
    return np.concatenate([part[:, None] < part[None, :], np.broadcast_to(np.arange(SLOTS), (P, SLOTS))],
                          axis=1).astype(np.float32)


def moe_parameters(b_router, b1):
    every = np.broadcast_to(b_router.reshape(1, N_EXPERTS), (P, N_EXPERTS))
    hidden = b1.reshape(N_EXPERTS, FC, P, 2).transpose(2, 0, 1, 3).reshape(P, -1)
    return np.concatenate([every, hidden], axis=1)


def moe_signals(ctx, nc, g):
    for name, per, base in (
        ("h_made", 1, 0), ("route_done", 1, 0), ("turned", 2, 0), ("turned_out", 2, 0), ("chosen", 1, 0),
        ("ranked", 1, 0), ("turns_set", 1, 0), ("gates_set", 1, 0), ("gates_turned", 1, 0), ("gates_out", 1, 0),
        ("zeros_set", 1, 0), ("top_set", 1, 0), ("odds_ready", 1, 0),
        ("e_unit", E_UNITS, E_UNITS), ("sel_ready", 1, 1), ("glu_ready", 2, 0), ("sig_ready", 2, 0), ("act_ready", 2, 0),
        ("gt_done", 1, 1), ("gt_out", 1, 1), ("ye_out", 2, 2), ("moe_step", 10, 0),
        ("acc_done", 1, 0), ("res_out", 4, 0), ("fin_sum", 2, 0), ("fin_squared", 1, 0), ("fin_root", 1, 0),
        ("x_done", 1, 0),
    ):
        g[name] = Signal(ctx, nc, name, per, 1, base)


def moe_memory(ctx, nc, g):
    def sb(name, shape, dt=F32, parts=P):
        g[name] = ctx.enter_context(nc.sbuf_tensor(name, [parts] + shape, dt))
        return g[name]

    more = sb("ring2", [E_UNITS - RING, DC, UNIT])
    g["slots"] = [g["ring"][:, i] for i in range(RING)] + [more[:, i] for i in range(E_UNITS - RING)]
    g["ec"] = lambda name: g["moec"][:, MOE_CONST[name][0]:MOE_CONST[name][1]]
    sb("b2", [D], parts=N_EXPERTS)
    sb("h3", [DC, T])
    sb("h_tok", [TC, D])
    sb("zero", [2 * T])
    for name in ("logit", "above", "equal", "count", "chosen_map", "gate_map", "rank", "odds"):
        sb(name, [TC, N_EXPERTS])
    sb("top", [TC, 8])
    sb("few", [TC, 4])
    sb("busy", [4])
    sb("turns", [1], mybir.dt.int32)
    sb("gT", [T], parts=N_EXPERTS)
    sb("sel", [TC, SLOTS])
    sb("selg", [TC, SLOTS])
    sb("selgT", [T], parts=SLOTS)
    sb("hsel", [DC, SLOTS])
    sb("glu", [FC // 2, SLOTS])
    sb("lin", [FC // 2, SLOTS])
    sb("sig", [FC // 2, SLOTS])
    sb("hid", [FC, SLOTS])
    sb("ye", [D], parts=SLOTS)
    sb("fin", [DC, T])
    sb("finrow", [2, T])


def moe_turns(eng, g):
    eng.wait_ge(g["turns_set"].sem, 1)
    return eng.value_load(g["turns"][0:1, 0:1], min_val=N_EXPERTS, max_val=N_EXPERTS * MAX_ROUNDS)


def moe_loads(sp, nc, g):
    def unit(e, j):
        src = g["w1"][0, bass.ds(e, 1), :, j * UNIT:(j + 1) * UNIT] if j < 4 else \
            g["w2"][0, bass.ds(e, 1), :, (j - 4) * UNIT:(j - 3) * UNIT]
        return sp.dma_start(g["slots"][j], src.rearrange("o (k p) n -> p (o k) n", p=P))

    for j in (1, 2, 0, 3, 4, 5):
        if j == 2:
            sp.wait_ge(g["mo_done"].sem, g["mo_done"].at(None, 4))
        if j == 3:
            sp.wait_ge(g["x_mixed"].sem, g["x_mixed"].at(None, 1))
        unit(0, j).then_inc(g["e_landed"][j].sem, g["e_landed"][j].unit)
    turns = moe_turns(sp, g)
    with sp.Fori(1, turns) as t:
        for j in range(E_UNITS):
            sp.wait_ge(g["e_unit"].sem, t * E_UNITS + (j + 1))
            unit(t % N_EXPERTS, j).then_inc(g["e_landed"][j].sem, g["e_landed"][j].one())


def moe_early_loads(pool, nc, g):
    a = MOE_CONST["b_router"][0]
    for dst, src in ((g["moec"][:, 0:a], g["moe_const_dram"]), (g["moec"][:, a:], g["moe_par_dram"]),
                     (g["wr"][:, :, :], g["w_router"][0].rearrange("(k p) e -> p k e", p=P))):
        pool.dma_start(dst, src).then_inc(g["moe_in"].sem, g["moe_in"].one())


def moe_pool(pool, nc, g):
    pool.wait_ge(g["x_mixed"].sem, g["x_mixed"].at(None, 1))
    pool.dma_start(g["b2"][:, :], g["b2_dram"][0]).then_inc(g["b2_in"].sem, g["b2_in"].one())


def moe_tensor(pe, nc, g):
    flat = [b[:, :, :].rearrange("p a b -> p (a b)") for b in g["bank"]]
    ident, ones, tri = g["c"]("ident"), g["c"]("ones"), g["ec"]("tri")
    pe.wait_ge(g["moe_in"].sem, g["moe_in"].at(None, 3))
    pe.wait_ge(g["h_made"].sem, g["h_made"].at(None, 1))
    for t in range(TC):
        for k in range(DC):
            mm = nc.tensor.matmul(flat[4][:, t * N_EXPERTS:(t + 1) * N_EXPERTS], g["h3"][:, k, t * P:(t + 1) * P],
                                  g["wr"][:, k, :], start=(k == 0), stop=(k == DC - 1))
    mm.then_inc(g["route_done"].sem, g["route_done"].one())
    for t in range(TC):
        for k in range(DC):
            mm = nc.tensor.transpose(flat[2 * t + k // 4][:, (k % 4) * P:(k % 4 + 1) * P],
                                     g["h3"][:, k, t * P:(t + 1) * P], ident)
        mm.then_inc(g["turned"].sem, g["turned"].one())
    pe.wait_ge(g["chosen"].sem, g["chosen"].at(None, 1))
    m = g["chosen_map"]
    nc.tensor.matmul(flat[5][:, 0:N_EXPERTS], tri, m[:, 0, :], start=True, stop=True)
    nc.tensor.matmul(flat[5][:, N_EXPERTS:2 * N_EXPERTS], ones, m[:, 0, :], start=True, stop=False)
    nc.tensor.matmul(flat[5][:, N_EXPERTS:2 * N_EXPERTS], tri, m[:, 1, :], start=False, stop=True)
    for t in range(TC):
        mm = nc.tensor.matmul(flat[5][:, 2 * N_EXPERTS:3 * N_EXPERTS], ones, m[:, t, :], start=(t == 0), stop=(t == 1))
    mm.then_inc(g["ranked"].sem, g["ranked"].one())
    pe.wait_ge(g["gates_set"].sem, g["gates_set"].at(None, 1))
    for t in range(TC):
        mm = nc.tensor.transpose(flat[6][0:N_EXPERTS, t * P:(t + 1) * P], g["gate_map"][:, t, :], ident)
    mm.then_inc(g["gates_turned"].sem, g["gates_turned"].one())
    pe.wait_ge(g["turned_out"].sem, g["turned_out"].at(None, 2))
    pe.wait_ge(g["zeros_set"].sem, g["zeros_set"].at(None, 1))
    for b in range(4):
        nc.tensor.matmul(flat[b], g["zero"][:, 0:P], g["zero"][:, :], start=True, stop=False, skip_group_check=True)

    def gather():
        for k in range(DC):
            b, at = (6, k) if k < BANK6 else (7, k - BANK6)
            for t in range(TC):
                mm = nc.tensor.matmul(flat[b][:, at * SLOTS:(at + 1) * SLOTS], g["h_tok"][:, t, k * P:(k + 1) * P],
                                      g["sel"][:, t, :], start=(t == 0), stop=(t == 1))
        return mm

    def scatter():
        for n in range(DC):
            nc.tensor.matmul(g["bank"][n // 2][:, n % 2, :], g["ye"][:, n * P:(n + 1) * P], g["selgT"][:, :],
                             start=False, stop=False, skip_group_check=True)

    pe.wait_ge(g["sel_ready"].sem, g["sel_ready"].at(None, 0))
    pe.wait_ge(g["gates_out"].sem, g["gates_out"].at(None, 1))
    gather().then_inc(g["gt_done"].sem, 1)
    turns = moe_turns(pe, g)
    pe.sem_inc(g["e_unit"].sem, E_UNITS)
    with pe.Fori(0, turns) as t:
        def landed(j):
            s = g["e_landed"][j]
            pe.wait_ge(s.sem, s.at(t, 1))
            return g["slots"][j]

        pe.wait_ge(g["gt_out"].sem, g["gt_out"].at(t, 0))
        for j in range(4):
            w = landed(j)
            for side in range(2):
                if j == 0:
                    pe.wait_ge(g["ye_out"].sem, g["ye_out"].at(t, side - 1))
                for i in range(2):
                    at = (2 * (j % 2) + i) * SLOTS
                    for k in range(DC):
                        mm = nc.tensor.matmul(flat[4 + 2 * (j // 2) + side][:, at:at + SLOTS],
                                              w[:, k, i * 2 * P + side:(i + 1) * 2 * P:2], g["hsel"][:, k, :],
                                              start=(k == 0), stop=(k == DC - 1))
            mm.then_inc(g["e_unit"].sem, g["e_unit"].one())
        scatter()

        def rows(n, k, w):
            return nc.tensor.matmul(flat[4 + n][0:SLOTS, :], g["hid"][:, k, :], w[:, k, :], start=(k == 0), stop=(k == FC - 1))

        pe.wait_ge(g["act_ready"].sem, g["act_ready"].at(t, 1))
        w = [landed(4), landed(5)]
        for n in range(2):
            for k in range(FC // 2):
                rows(n, k, w[n])
        pe.wait_ge(g["act_ready"].sem, g["act_ready"].at(t, 2))
        for k in range(FC // 2, FC):
            mm = rows(0, k, w[0])
        mm.then_inc(g["e_unit"].sem, g["e_unit"].one())
        pe.wait_ge(g["sel_ready"].sem, g["sel_ready"].at(t, 1))
        gather()
        for i in range(TC):
            mm = nc.tensor.transpose(flat[7][0:SLOTS, T + i * P:T + (i + 1) * P], g["selg"][:, i, :], ident)
        mm.then_inc(g["gt_done"].sem, g["gt_done"].one())
        for k in range(FC // 2, FC):
            mm = rows(1, k, w[1])
        mm.then_inc(g["e_unit"].sem, g["e_unit"].one())
    pe.wait_ge(g["all_out"].sem, 1)
    scatter()
    pe.wait_ge(g["b2_in"].sem, g["b2_in"].at(None, 1))
    for n in range(DC):
        mm = nc.tensor.matmul(g["bank"][n // 2][:, n % 2, :], g["b2"][:, n * P:(n + 1) * P], g["gT"][:, :],
                              start=False, stop=True, skip_group_check=True)
    mm.then_inc(g["acc_done"].sem, g["acc_done"].one())
    pe.wait_ge(g["res_out"].sem, g["res_out"].at(None, 4))
    for c in range(DC):
        mm = nc.tensor.matmul(g["bank"][4][:, 0, :], ones, g["xT"][:, c, :], start=(c == 0), stop=(c == DC - 1))
    mm.then_inc(g["fin_sum"].sem, g["fin_sum"].one())
    pe.wait_ge(g["fin_squared"].sem, g["fin_squared"].at(None, 1))
    for c in range(DC):
        mm = nc.tensor.matmul(g["bank"][5][:, 0, :], ones, g["fin"][:, c, :], start=(c == 0), stop=(c == DC - 1))
    mm.then_inc(g["fin_sum"].sem, g["fin_sum"].one())


def moe_scalar(act, nc, g):
    flat = [b[:, :, :].rearrange("p a b -> p (a b)") for b in g["bank"]]
    for t in range(TC):
        act.wait_ge(g["turned"].sem, g["turned"].at(None, t + 1))
        for b in range(2):
            ins = nc.scalar.activation(g["h_tok"][:, t, b * UNIT:(b + 1) * UNIT], flat[2 * t + b], ACT.Copy)
        ins.then_inc(g["turned_out"].sem, g["turned_out"].one())
    act.wait_ge(g["top_set"].sem, g["top_set"].at(None, 1))
    for t in range(TC):
        ins = nc.scalar.activation(g["odds"][:, t, :], g["logit"][:, t, :], ACT.Exp, bias=g["few"][:, t, 0:1])
    ins.then_inc(g["odds_ready"].sem, g["odds_ready"].one())
    act.wait_ge(g["gates_turned"].sem, g["gates_turned"].at(None, 1))
    nc.scalar.activation(g["gT"][:, :], flat[6][0:N_EXPERTS, 0:T], ACT.Copy).then_inc(
        g["gates_out"].sem, g["gates_out"].one())

    def take_rows():
        nc.scalar.activation(g["hsel"][:, 0:BANK6, :], flat[6][:, 0:BANK6 * SLOTS].rearrange("p (k s) -> p k s", s=SLOTS),
                             ACT.Copy)
        return nc.scalar.activation(g["hsel"][:, BANK6:DC, :],
                                    flat[7][:, 0:BANK7 * SLOTS].rearrange("p (k s) -> p k s", s=SLOTS), ACT.Copy)

    act.wait_ge(g["gt_done"].sem, g["gt_done"].at(None, 0))
    take_rows().then_inc(g["gt_out"].sem, 1)
    act.wait_ge(g["zeros_set"].sem, g["zeros_set"].at(None, 1))
    act.sem_inc(g["ye_out"].sem, 2)
    turns = moe_turns(act, g)
    with act.Fori(0, turns) as t:
        for h in range(2):
            act.wait_ge(g["glu_ready"].sem, g["glu_ready"].at(t, h + 1))
            nc.scalar.activation(g["sig"][:, :, :], g["glu"][:, :, :], ACT.Sigmoid, scale=SIG_ALPHA).then_inc(
                g["sig_ready"].sem, g["sig_ready"].one())
        act.wait_ge(g["e_unit"].sem, g["e_unit"].at(t, 5))
        nc.scalar.activation(g["ye"][:, 0:UNIT], flat[4][0:SLOTS, :], ACT.Copy).then_inc(
            g["ye_out"].sem, g["ye_out"].one())
        act.wait_ge(g["gt_done"].sem, g["gt_done"].at(t, 1))
        take_rows()
        nc.scalar.activation(g["selgT"][:, :], flat[7][0:SLOTS, T:2 * T], ACT.Copy).then_inc(
            g["gt_out"].sem, g["gt_out"].one())
        act.wait_ge(g["e_unit"].sem, g["e_unit"].at(t, 6))
        nc.scalar.activation(g["ye"][:, UNIT:D], flat[5][0:SLOTS, :], ACT.Copy).then_inc(
            g["ye_out"].sem, g["ye_out"].one())
    nc.scalar.activation(g["finrow"][0:1, 0, 0:1], g["zero"][0:1, 0:1], ACT.Copy).then_inc(g["all_out"].sem, 1)
    act.wait_ge(g["fin_sum"].sem, g["fin_sum"].at(None, 2))
    nc.scalar.activation(g["finrow"][:, 0, :], g["bank"][5][:, 0, :], ACT.Sqrt, bias=g["eps3"][:, 0:1], scale=1.0 / D).then_inc(
        
        g["fin_root"].sem, g["fin_root"].one())


def moe_vector(dve, nc, g):
    v = nc.vector
    flat = [b[:, :, :].rearrange("p a b -> p (a b)") for b in g["bank"]]
    mp, mod, xT = g["mpar"], g["mod"], g["xT"]
    steps = g["e_dve"]

    for name in ("zero", "ye", "selgT"):
        v.memset(g[name][:, :], 0.0)
    ins = v.memset(g["eps3"][:, :], LN_EPS)
    ins.then_inc(g["zeros_set"].sem, g["zeros_set"].one())
    for c in range(DC):
        ins = v.tensor_scalar(g["h3"][:, c, :], xT[:, c, :], mod[:, SC2 + c, 0:1], mod[:, SH2 + c, 0:1], ALU.mult, ALU.add)
    ins.then_inc(g["h_made"].sem, g["h_made"].one())
    logit, top, few = g["logit"], g["top"], g["few"]
    dve.wait_ge(g["moe_in"].sem, g["moe_in"].at(None, 3))
    dve.wait_ge(g["route_done"].sem, g["route_done"].at(None, 1))
    v.tensor_tensor(logit[:, :, :], flat[4][:, 0:TC * N_EXPERTS].rearrange("p (t e) -> p t e", t=TC),
                    row(g["ec"]("b_router"), TC), ALU.add).then_inc(g["e_dve"].sem, g["e_dve"].one())
    dve.wait_ge(g["e_dve"].sem, g["e_dve"].now(None))
    for t in range(TC):
        ins = v.max(top[:, t, :], logit[:, t, :])
    ins.then_inc(g["e_dve"].sem, g["e_dve"].one())
    dve.wait_ge(g["e_dve"].sem, g["e_dve"].now(None))
    v.tensor_scalar(few[:, :, 0:1], top[:, :, 0:1], -1.0, None, ALU.mult).then_inc(g["top_set"].sem, g["top_set"].one())
    for t in range(TC):
        v.tensor_scalar(g["above"][:, t, :], logit[:, t, :], top[:, t, TOP_K - 1:TOP_K], None, ALU.is_gt)
        ins = v.tensor_scalar(g["equal"][:, t, :], logit[:, t, :], top[:, t, TOP_K - 1:TOP_K], None, ALU.is_equal)
    ins.then_inc(g["e_dve"].sem, g["e_dve"].one())
    dve.wait_ge(g["e_dve"].sem, g["e_dve"].now(None))
    v.tensor_reduce(few[:, :, 1:2], g["above"][:, :, :], AX_X, ALU.add)
    for t in range(TC):
        ins = v.tensor_tensor_scan(g["count"][:, t, :], g["c"]("ones")[:, 0:N_EXPERTS], g["equal"][:, t, :], 0.0,
                                   ALU.mult, ALU.add)
    ins.then_inc(g["e_dve"].sem, g["e_dve"].one())
    dve.wait_ge(g["e_dve"].sem, g["e_dve"].now(None))
    for t in range(TC):
        ins = v.tensor_scalar(g["count"][:, t, :], g["count"][:, t, :], few[:, t, 1:2], float(TOP_K), ALU.add, ALU.is_le)
    ins.then_inc(g["e_dve"].sem, g["e_dve"].one())
    dve.wait_ge(g["e_dve"].sem, g["e_dve"].now(None))
    v.tensor_tensor(g["equal"][:, :, :], g["equal"][:, :, :], g["count"][:, :, :], ALU.mult).then_inc(
        g["e_dve"].sem, g["e_dve"].one())
    dve.wait_ge(g["e_dve"].sem, g["e_dve"].now(None))
    v.tensor_tensor(g["chosen_map"][:, :, :], g["above"][:, :, :], g["equal"][:, :, :], ALU.add).then_inc(
        g["chosen"].sem, g["chosen"].one())
    dve.wait_ge(g["chosen"].sem, g["chosen"].at(None, 1))
    dve.wait_ge(g["odds_ready"].sem, g["odds_ready"].at(None, 1))
    v.tensor_tensor(g["odds"][:, :, :], g["odds"][:, :, :], g["chosen_map"][:, :, :], ALU.mult).then_inc(
        g["e_dve"].sem, g["e_dve"].one())
    dve.wait_ge(g["e_dve"].sem, g["e_dve"].now(None))
    v.tensor_reduce(few[:, :, 2:3], g["odds"][:, :, :], AX_X, ALU.add).then_inc(g["e_dve"].sem, g["e_dve"].one())
    dve.wait_ge(g["e_dve"].sem, g["e_dve"].now(None))
    v.reciprocal(few[:, :, 3:4], few[:, :, 2:3]).then_inc(g["e_dve"].sem, g["e_dve"].one())
    dve.wait_ge(g["e_dve"].sem, g["e_dve"].now(None))
    for t in range(TC):
        ins = v.tensor_scalar(g["gate_map"][:, t, :], g["odds"][:, t, :], few[:, t, 3:4], None, ALU.mult)
    ins.then_inc(g["gates_set"].sem, g["gates_set"].one())
    dve.wait_ge(g["ranked"].sem, g["ranked"].at(None, 1))
    v.scalar_tensor_tensor(out=g["rank"][:, :, :], in0=flat[5][:, 0:TC * N_EXPERTS].rearrange("p (t e) -> p t e", t=TC),
                           scalar=1.0, in1=g["chosen_map"][:, :, :], op0=ALU.add, op1=ALU.mult).then_inc(
        g["e_dve"].sem, g["e_dve"].one())
    dve.wait_ge(g["e_dve"].sem, g["e_dve"].now(None))
    v.tensor_scalar(g["rank"][:, :, :], g["rank"][:, :, :], -1.0, None, ALU.add)
    busy = g["busy"]
    v.tensor_reduce(busy[:, 0:1], flat[5][:, 2 * N_EXPERTS:3 * N_EXPERTS], AX_X, ALU.max).then_inc(
        g["e_dve"].sem, g["e_dve"].one())
    dve.wait_ge(g["e_dve"].sem, g["e_dve"].now(None))
    for r in range(1, MAX_ROUNDS):
        ins = v.tensor_scalar(busy[:, r:r + 1], busy[:, 0:1], float(r * SLOTS), float(N_EXPERTS), ALU.is_gt, ALU.mult)
    ins.then_inc(g["e_dve"].sem, g["e_dve"].one())
    dve.wait_ge(g["e_dve"].sem, g["e_dve"].now(None))
    v.tensor_reduce(busy[:, 0:1], busy[:, 1:MAX_ROUNDS], AX_X, ALU.add).then_inc(g["e_dve"].sem, g["e_dve"].one())
    dve.wait_ge(g["e_dve"].sem, g["e_dve"].now(None))
    v.tensor_scalar(g["turns"][:, :], busy[:, 0:1], float(N_EXPERTS), None, ALU.add).then_inc(
        g["turns_set"].sem, g["turns_set"].one())

    def choose(out, e, gated):
        for t in range(TC):
            where = g["rank"][:, t, bass.ds(e, 1)]
            if gated:
                ins = v.tensor_scalar(out[:, t, :], g["ec"]("slot"), where, g["gate_map"][:, t, bass.ds(e, 1)],
                                      ALU.is_equal, ALU.mult)
            else:
                ins = v.tensor_scalar(out[:, t, :], g["ec"]("slot"), where, None, ALU.is_equal)
        return ins

    choose(g["sel"], 0, False).then_inc(g["sel_ready"].sem, 1)
    turns = moe_turns(dve, g)
    glu, lin, b1 = g["glu"], g["lin"], g["ec"]("b1").rearrange("p (e c s) -> p e c s", e=N_EXPERTS, s=2)
    with dve.Fori(0, turns) as t:
        e, after = t % N_EXPERTS, (t + 1) % N_EXPERTS

        dve.wait_ge(g["e_unit"].sem, g["e_unit"].at(t, 1))
        choose(g["selg"], e, True).then_inc(g["moe_step"].sem, g["moe_step"].one())
        dve.wait_ge(g["moe_step"].sem, g["moe_step"].now(t))
        left = g["rank"][:, :, bass.ds(e, 1)]
        v.tensor_scalar(left, left, float(-SLOTS), None, ALU.add).then_inc(g["moe_step"].sem, g["moe_step"].one())
        dve.wait_ge(g["moe_step"].sem, g["moe_step"].now(t))
        choose(g["sel"], after, False).then_inc(g["sel_ready"].sem, g["sel_ready"].one())
        for h in range(2):
            dve.wait_ge(g["e_unit"].sem, g["e_unit"].at(t, 2 * h + 2))
            n = FC // 2

            def bias(side):
                return b1[:, bass.ds(e, 1), h * n:(h + 1) * n, side].rearrange("p o c -> p (o c)").unsqueeze(2) \
                    .to_broadcast([P, n, SLOTS])

            def hidden(side):
                return flat[4 + 2 * h + side][:, 0:n * SLOTS].rearrange("p (c s) -> p c s", s=SLOTS)

            v.tensor_tensor(glu[:, :, :], hidden(0), bias(0), ALU.add).then_inc(g["moe_step"].sem, g["moe_step"].one())
            dve.wait_ge(g["moe_step"].sem, g["moe_step"].now(t))
            v.tensor_scalar(glu[:, :, :], glu[:, :, :], LIMIT, None, ALU.min).then_inc(
                g["glu_ready"].sem, g["glu_ready"].one())
            v.tensor_tensor(lin[:, :, :], hidden(1), bias(1), ALU.add).then_inc(g["moe_step"].sem, g["moe_step"].one())
            dve.wait_ge(g["moe_step"].sem, g["moe_step"].now(t))
            v.tensor_scalar(lin[:, :, :], lin[:, :, :], -LIMIT, LIMIT, ALU.max, ALU.min).then_inc(
                g["moe_step"].sem, g["moe_step"].one())
            dve.wait_ge(g["moe_step"].sem, g["moe_step"].now(t))
            v.scalar_tensor_tensor(out=lin[:, :, :], in0=lin[:, :, :], scalar=1.0, in1=glu[:, :, :], op0=ALU.add,
                                   op1=ALU.mult).then_inc(g["moe_step"].sem, g["moe_step"].one())
            dve.wait_ge(g["moe_step"].sem, g["moe_step"].now(t))
            dve.wait_ge(g["sig_ready"].sem, g["sig_ready"].at(t, h + 1))
            v.tensor_tensor(g["hid"][:, h * n:(h + 1) * n, :], lin[:, :, :], g["sig"][:, :, :], ALU.mult).then_inc(
                g["act_ready"].sem, g["act_ready"].one())
    dve.wait_ge(g["acc_done"].sem, g["acc_done"].at(None, 1))
    fin = g["fin"]
    for i in range(4):
        for j in range(2):
            c = 2 * i + j
            ins = v.tensor_scalar(fin[:, c, :], g["bank"][i][:, j, :], mod[:, GT2 + c, 0:1], None, ALU.mult)
        ins.then_inc(g["e_dve"].sem, g["e_dve"].one())
        dve.wait_ge(g["e_dve"].sem, g["e_dve"].now(None))
        both = xT[:, 2 * i:2 * i + 2, :]
        v.scalar_tensor_tensor(out=both, in0=both, scalar=ALPHA, in1=fin[:, 2 * i:2 * i + 2, :], op0=ALU.mult,
                               op1=ALU.add).then_inc(g["res_out"].sem, g["res_out"].one())
    dve.wait_ge(g["fin_sum"].sem, g["fin_sum"].at(None, 1))
    v.tensor_scalar(g["finrow"][:, 1, :], g["bank"][4][:, 0, :], 1.0 / D, None, ALU.mult).then_inc(
        g["e_dve"].sem, g["e_dve"].one())
    dve.wait_ge(g["e_dve"].sem, g["e_dve"].now(None))
    v.tensor_tensor(xT[:, :, :], xT[:, :, :], row(g["finrow"][:, 1, :], DC), ALU.subtract).then_inc(
        g["e_dve"].sem, g["e_dve"].one())
    dve.wait_ge(g["e_dve"].sem, g["e_dve"].now(None))
    v.tensor_tensor(fin[:, :, :], xT[:, :, :], xT[:, :, :], ALU.mult).then_inc(
        g["fin_squared"].sem, g["fin_squared"].one())
    dve.wait_ge(g["fin_root"].sem, g["fin_root"].at(None, 1))
    v.reciprocal(g["finrow"][:, 0, :], g["finrow"][:, 0, :]).then_inc(g["e_dve"].sem, g["e_dve"].one())
    dve.wait_ge(g["e_dve"].sem, g["e_dve"].now(None))
    v.tensor_tensor(xT[:, :, :], xT[:, :, :], row(g["finrow"][:, 0, :], DC), ALU.mult).then_inc(
        g["e_dve"].sem, g["e_dve"].one())
    dve.wait_ge(g["e_dve"].sem, g["e_dve"].now(None))
    for c in range(DC):
        a, b = MIX_PAR["ln2_g"] + c, MIX_PAR["ln2_b"] + c
        ins = v.tensor_scalar(xT[:, c, :], xT[:, c, :], mp[:, a:a + 1], mp[:, b:b + 1], ALU.mult, ALU.add)
    ins.then_inc(g["x_done"].sem, g["x_done"].one())


INIT_DVE = 49


def mixer_units(i):
    return len(range(i, B_UNITS, RING))


def program(nc, w, out):
    with ExitStack() as ctx:
        shared = dict(w)
        shared["bank"] = [ctx.enter_context(nc.psum_tensor(f"bank{i}", [P, 2, T], F32)) for i in range(8)]
        for name, shape in (("ring", [RING, DC, UNIT]), ("xT", [DC, T]), ("shared_cons", [3 * P]), ("mod", [6 * DC, 2]),
                            ("mpar", [MIX_PAR_WIDTH]), ("cond", [DC, 2]), ("eps3", [1])):
            shared[name] = ctx.enter_context(nc.sbuf_tensor(name, [P] + shape, F32))
        shared["c"] = lambda name: shared["shared_cons"][:, CONST[name][0]:CONST[name][1]]
        shared["x_mixed"] = Signal(ctx, nc, "x_mixed", 1)
        start_in = Signal(ctx, nc, "start_in", 4, 16)
        eps_set = Signal(ctx, nc, "eps_set", 1)
        out_done = Signal(ctx, nc, "out_done", 1, 16)

        hyb = dict(shared)
        with ExitStack() as scope:
            hyb["hT"] = scope.enter_context(nc.sbuf_tensor("hT", [P, DC, T], F32))
            hybrid_memory(scope, nc, hyb)
        hyb["c"] = lambda name: hyb["cons"][:, CONST[name][0]:CONST[name][1]]
        hybrid_signals(ctx, nc, hyb)

        for name, shape in (("moec", [MOE_CONST_WIDTH]), ("wr", [DC, N_EXPERTS])):
            shared[name] = ctx.enter_context(nc.sbuf_tensor(name, [P] + shape, F32))
        mix = dict(shared)
        mix["y_done"], mix["y_out"] = hyb["y_done"], hyb["y_out"]
        with ExitStack() as scope:
            mixer_memory(scope, nc, mix)
        mixer_aliases(mix)
        mixer_signals(ctx, nc, mix)
        mix["wf_zero"] = Signal(ctx, nc, "wf_zero", 1)
        mix["landed_b"] = [follow(s, DEPTH * s.per, mixer_units(i)) for i, s in enumerate(hyb["landed"])]
        mix["init_dve"] = follow(hyb["dve_step"], DEPTH * hyb["dve_step"].per, INIT_DVE)

        moe = dict(shared)
        moe["mo_done"] = mix["mo_done"]
        with ExitStack() as scope:
            moe_memory(scope, nc, moe)
        moe_signals(ctx, nc, moe)
        moe["e_landed"] = [follow(s, s.per, 1) for s in mix["landed_b"]] \
            + [Signal(ctx, nc, f"landed{i}", 1, 16) for i in range(RING, E_UNITS)]
        moe["moe_in"] = Signal(ctx, nc, "moe_in", 3, 16)
        moe["b2_in"] = Signal(ctx, nc, "b2_in", 1, 16)
        moe["e_dve"] = follow(mix["init_dve"], INIT_DVE, None)
        moe["all_out"] = Signal(ctx, nc, "all_out", None)

        block = ctx.enter_context(nc.Block())

        @block.sync
        def _(sp):
            sp.dma_start(shared["xT"][:, :, :], shared["x"]).then_inc(start_in.sem, start_in.one())
            sp.dma_start(shared["shared_cons"][:, :], shared["cons_dram"][:, 0:3 * P]).then_inc(
                start_in.sem, start_in.one())
            sp.dma_start(hyb["cons"][:, :], shared["cons_dram"]).then_inc(start_in.sem, start_in.one())
            sp.dma_start(shared["mpar"][:, :], shared["mpar_dram"]).then_inc(start_in.sem, start_in.one())
            with sp.Fori(0, DEPTH) as l:
                hybrid_loads(sp, nc, hyb, l)
            mixer_loads(sp, nc, mix)
            moe_loads(sp, nc, moe)
            sp.wait_ge(moe["x_done"].sem, 1)
            sp.dma_start(out, shared["xT"][:, :, :]).then_inc(out_done.sem, out_done.one())
            sp.wait_ge(out_done.sem, out_done.at(None, 1))

        @block.gpsimd
        def _(pool):
            with pool.Fori(0, DEPTH) as l:
                hybrid_pool(pool, nc, hyb, l)
            mixer_pool(pool, nc, mix, moe)
            moe_pool(pool, nc, moe)

        @block.scalar
        def _(act):
            act.wait_ge(eps_set.sem, 1)
            act.wait_ge(start_in.sem, start_in.at(None, 4))
            nc.scalar.activation(shared["cond"][:, :, :].rearrange("p a b -> p (a b)"),
                                 shared["mpar"][:, MIX_PAR["cond"]:MIX_PAR["cond"] + 2 * DC], ACT.Silu).then_inc(
                mix["cond_ready"].sem, mix["cond_ready"].one())
            with act.Fori(0, DEPTH) as l:
                hybrid_scalar(act, nc, hyb, l)
            mixer_scalar(act, nc, mix)
            moe_scalar(act, nc, moe)

        @block.vector
        def _(dve):
            nc.vector.memset(hyb["eps"][:, :], EPS).then_inc(eps_set.sem, eps_set.one())
            dve.sem_inc(hyb["y_out"].sem, hyb["y_out"].base)
            dve.wait_ge(start_in.sem, start_in.at(None, 4))
            with dve.Fori(0, DEPTH) as l:
                hybrid_vector(dve, nc, hyb, l)
            mixer_vector(dve, nc, mix)
            moe_vector(dve, nc, moe)

        @block.tensor
        def _(pe):
            pe.sem_inc(hyb["y_done"].sem, hyb["y_done"].base)
            pe.wait_ge(start_in.sem, start_in.at(None, 4))
            with pe.Fori(0, DEPTH) as l:
                hybrid_tensor(pe, nc, hyb, l)
            mixer_tensor(pe, nc, mix)
            moe_tensor(pe, nc, moe)

        every = [s for g in (hyb, mix, moe) for s in g.values() if isinstance(s, Signal)]
        wrong = [(s.name, s.n, s.per) for s in every if s.per is not None and s.n != s.per]
        assert not wrong, wrong


def kernel(**inputs):
    import concourse.bacc as _bacc
    from concourse.bass_utils import run_bass_kernel_spmd as _run

    nc = _bacc.Bacc("TRN2", target_bir_lowering=False, num_devices=1)
    i = {k: np.asarray(v) for k, v in inputs.items()}

    def down(a):
        return np.ascontiguousarray(a[0].T.reshape(DC, P, T).transpose(1, 0, 2))

    arrays = {k: i[k] for k in ("w_in", "w_conv_out", "w_ret_out", "w_attn_out", "w_out")}
    arrays |= {"w_ada": i["w_ada_2"], "w_in2": i["w_in_2"], "w_out2": i["w_out_2"], "w2_decay": i["w2_decay_2"],
               "a2_iclr": i["a2_iclr_2"], "g2_gate": i["g2_gate_2"], "w_fno": i["w_fno_2"],
               "w_router": i["w_router_2"], "w1": i["w1_2"], "w2": i["w2_2"], "b2_dram": i["b2_2"]}
    arrays["x"], arrays["ctxT"] = down(i["x"]), down(i["ctx_2"])
    arrays["cons_dram"] = hybrid_constants()
    arrays["par_dram"] = np.ascontiguousarray(hybrid_parameters(*(i[k] for k in (
        "norm_g", "b_gate", "conv_b", "conv_ln_g", "conv_ln_b", "conv_dw", "ret_decay", "q_norm_g", "k_norm_g", "attn_sink"))))
    arrays["mcons_dram"] = mixer_constants()
    arrays["mpar_dram"] = np.ascontiguousarray(mixer_parameters(*(i[k + "_2"] for k in (
        "ln0_g", "ln0_b", "b_ada", "mu_shift", "w0", "a0", "r_k", "k_k", "k_a", "gn_g", "gn_b", "b_fno", "ln1_g", "ln1_b",
        "ln2_g", "ln2_b", "c", "c_ctx"))))
    arrays["moe_const_dram"] = moe_constants()
    arrays["moe_par_dram"] = np.ascontiguousarray(moe_parameters(i["b_router_2"], i["b1_2"]))
    w = {k: nc.dram_tensor(f"in_{k}", a.shape, F32, kind="ExternalInput").ap() for k, a in arrays.items()}
    out = nc.dram_tensor("out_x", (P, DC, T), F32, kind="ExternalOutput").ap()
    program(nc, w, out)
    r = _run(nc, [{f"in_{k}": a for k, a in arrays.items()}], core_ids=[0])
    got = r.results[0]["out_x"]
    return np.ascontiguousarray(got.transpose(1, 0, 2).reshape(D, T).T)[None]
```
